# Optimizing a Trainium2 kernel written in Bass

```python
import jax, jax.numpy as jnp
from jax import lax
import numpy as np

D_MODEL = 1024
BATCH = 1
SEQ = 128
DEPTH = 2
DEC_BATCH = 1
DEC_SEQ = 512
PAST_LEN = 256

GRID_W = 64
HEAD_DIM = 64
N_Q_HEADS = 8
N_KV_HEADS = 2
GQA_GROUP = N_Q_HEADS // N_KV_HEADS
ATTN_WIDTH = N_Q_HEADS * HEAD_DIM
KV_WIDTH = N_KV_HEADS * HEAD_DIM
CONV_WIDTH = D_MODEL // 2
CONV_K = 3
POOL_WIDTH = D_MODEL // 2
POOL_WINDOWS = (2, 4, 8, 16)
POOL_GROUP = POOL_WIDTH // len(POOL_WINDOWS)
MIX_WIDTH = CONV_WIDTH + ATTN_WIDTH
EVEN_IN = 3 * CONV_WIDTH + ATTN_WIDTH + 2 * KV_WIDTH
ODD_IN = ATTN_WIDTH + 2 * KV_WIDTH + POOL_WIDTH
EVEN_SPLITS = (CONV_WIDTH, 2 * CONV_WIDTH, 3 * CONV_WIDTH, 3 * CONV_WIDTH + ATTN_WIDTH, 3 * CONV_WIDTH + ATTN_WIDTH + KV_WIDTH)
ODD_SPLITS = (ATTN_WIDTH, ATTN_WIDTH + KV_WIDTH, ATTN_WIDTH + 2 * KV_WIDTH)
Q_BLOCK = 128
WINDOW = 128
D_FF = 2816
N_EXPERTS = 8
TOP_K = 2
D_FF_EXPERT = 1024
ROPE_THETA = 10000.0
EPS = 1e-6
N_EVEN = (DEPTH + 1) // 2
N_ODD = DEPTH // 2

kernel_name = 'hybrid_flow_prefix_trunk'

def rms_norm(x, g):
    xf = x.astype(jnp.float32)
    y = xf * lax.rsqrt(jnp.mean(xf * xf, axis=-1, keepdims=True) + EPS)
    return (y * g.astype(jnp.float32)).astype(x.dtype)

def modulation(cond, w_mod, b_mod):
    m = jax.nn.silu(cond) @ w_mod + b_mod
    return jnp.split(m[:, None, :], 6, axis=-1)

def axial_rope_tables(n_tokens):
    n_rows = n_tokens // GRID_W
    rows = jnp.repeat(jnp.arange(n_rows, dtype=jnp.float32), GRID_W)
    cols = jnp.tile(jnp.arange(GRID_W, dtype=jnp.float32), n_rows)
    quarter = HEAD_DIM // 4
    inv = ROPE_THETA ** (-jnp.arange(quarter, dtype=jnp.float32) / quarter)
    ang = jnp.stack([rows[:, None] * inv, cols[:, None] * inv], axis=1)
    return jnp.cos(ang), jnp.sin(ang)

def apply_axial_rope(x, cos, sin):
    shp = x.shape
    xs = x.reshape(shp[:-1] + (2, 2, HEAD_DIM // 4)).astype(jnp.float32)
    x1, x2 = xs[..., 0, :], xs[..., 1, :]
    out = jnp.stack([x1 * cos - x2 * sin, x2 * cos + x1 * sin], axis=-2)
    return out.reshape(shp).astype(x.dtype)

def split_q(t):
    b, s, _ = t.shape
    return t.reshape(b, s, N_KV_HEADS, GQA_GROUP, HEAD_DIM).transpose(0, 2, 3, 1, 4)

def split_kv(t):
    b, s, _ = t.shape
    return t.reshape(b, s, N_KV_HEADS, HEAD_DIM).transpose(0, 2, 1, 3)

def merge_heads(o):
    b, kh, g, s, hd = o.shape
    return o.transpose(0, 3, 1, 2, 4).reshape(b, s, kh * g * hd)

def qkv_heads(q, k, v, q_gain, k_gain, rope):
    q = rms_norm(split_q(q), q_gain)
    k = rms_norm(split_kv(k), k_gain)
    v = split_kv(v)
    if rope is not None:
        cos, sin = rope
        q = apply_axial_rope(q, cos, sin)
        k = apply_axial_rope(k, cos, sin)
    return q, k, v

def attn_probs(s, sink):
    if sink is None:
        return jax.nn.softmax(s, axis=-1)
    sk = sink.astype(jnp.float32).reshape((1, N_KV_HEADS, GQA_GROUP) + (1,) * (s.ndim - 3))
    m = jnp.maximum(jnp.max(s, axis=-1, keepdims=True), sk)
    e = jnp.exp(s - m)
    return e / (jnp.sum(e, axis=-1, keepdims=True) + jnp.exp(sk - m))

def blocked_attention(q, k, v, sink=None):
    b, kh, g, sq, hd = q.shape
    nb = sq // Q_BLOCK
    qb = jnp.moveaxis(q.reshape(b, kh, g, nb, Q_BLOCK, hd), 3, 0)
    scale = HEAD_DIM ** -0.5

    def one_block(qi):
        s = jnp.einsum('bkgqd,bksd->bkgqs', qi, k, preferred_element_type=jnp.float32) * scale
        p = attn_probs(s, sink)
        return jnp.einsum('bkgqs,bksd->bkgqd', p.astype(v.dtype), v)

    out = lax.map(one_block, qb)
    return jnp.moveaxis(out, 0, 3).reshape(b, kh, g, sq, hd)

def banded_window_attention(q, k, v, k_ctx, v_ctx, sink):
    b, kh, g, s, hd = q.shape
    nb = s // Q_BLOCK
    n_ctx = k_ctx.shape[2]
    pad = ((0, 0), (0, 0), (Q_BLOCK, Q_BLOCK), (0, 0))
    kp = jnp.pad(k, pad).reshape(b, kh, nb + 2, Q_BLOCK, hd)
    vp = jnp.pad(v, pad).reshape(b, kh, nb + 2, Q_BLOCK, hd)
    kw = jnp.concatenate([kp[:, :, :-2], kp[:, :, 1:-1], kp[:, :, 2:]], axis=3)
    vw = jnp.concatenate([vp[:, :, :-2], vp[:, :, 1:-1], vp[:, :, 2:]], axis=3)
    qb = q.reshape(b, kh, g, nb, Q_BLOCK, hd)
    scale = HEAD_DIM ** -0.5
    s_loc = jnp.einsum('bkgnqd,bknwd->bkgnqw', qb, kw, preferred_element_type=jnp.float32) * scale
    qi = jnp.arange(nb)[:, None] * Q_BLOCK + jnp.arange(Q_BLOCK)[None, :]
    kj = jnp.arange(nb)[:, None] * Q_BLOCK - Q_BLOCK + jnp.arange(3 * Q_BLOCK)[None, :]
    valid = (jnp.abs(qi[:, :, None] - kj[:, None, :]) <= WINDOW) & (kj[:, None, :] >= 0) & (kj[:, None, :] < s)
    s_loc = jnp.where(valid, s_loc, -jnp.inf)
    s_ctx = jnp.einsum('bkgnqd,bkld->bkgnql', qb, k_ctx, preferred_element_type=jnp.float32) * scale
    p = attn_probs(jnp.concatenate([s_ctx, s_loc], axis=-1), sink).astype(v.dtype)
    out = (jnp.einsum('bkgnql,bkld->bkgnqd', p[..., :n_ctx], v_ctx)
           + jnp.einsum('bkgnqw,bknwd->bkgnqd', p[..., n_ctx:], vw))
    return out.reshape(b, kh, g, s, hd)

def multiscale_pool(x, pool_w, pool_scale):
    b, s, _ = x.shape
    xf = x.astype(jnp.float32)
    cs = jnp.pad(jnp.cumsum(xf, axis=1), ((0, 0), (1, 0), (0, 0)))
    t = jnp.arange(s)
    outs = []
    for gi, w in enumerate(POOL_WINDOWS):
        lo = jnp.clip(t - w // 2, 0, s)
        hi = jnp.clip(t - w // 2 + w, 0, s)
        sl = slice(gi * POOL_GROUP, (gi + 1) * POOL_GROUP)
        seg = cs[:, :, sl]
        cnt = (hi - lo).astype(jnp.float32)[None, :, None]
        outs.append((seg[:, hi] - seg[:, lo]) / cnt - xf[:, :, sl])
    d = jnp.stack(outs, axis=2)
    y = jnp.einsum('bsgc,gcd->bsgd', d, pool_w.astype(jnp.float32)).reshape(b, s, POOL_WIDTH)
    return (y * pool_scale.astype(jnp.float32)).astype(x.dtype)

def even_mixer(h, w_in, conv_w, q_gain, k_gain, w_out, ctx_kv, rope):
    z = h @ w_in
    bg, cg, xa, q, k, v = jnp.split(z, EVEN_SPLITS, axis=-1)
    u = jnp.pad(cg * xa, ((0, 0), (1, 1), (0, 0)))
    ya = bg * (u[:, :-2] * conv_w[0] + u[:, 1:-1] * conv_w[1] + u[:, 2:] * conv_w[2])
    qh, kh, vh = qkv_heads(q, k, v, q_gain, k_gain, rope)
    if ctx_kv is None:
        o = blocked_attention(qh, kh, vh)
        new_kv = (kh, vh)
    else:
        kc, vc = ctx_kv
        o = blocked_attention(qh, jnp.concatenate([kc, kh], axis=2), jnp.concatenate([vc, vh], axis=2))
        new_kv = None
    y = jnp.concatenate([ya, merge_heads(o)], axis=-1) @ w_out
    return y, new_kv

def odd_mixer(h, w_in, q_gain, k_gain, sink, pool_w, pool_scale, w_out, ctx_kv, rope):
    z = h @ w_in
    q, k, v, xd = jnp.split(z, ODD_SPLITS, axis=-1)
    qh, kh, vh = qkv_heads(q, k, v, q_gain, k_gain, rope)
    if ctx_kv is None:
        o = blocked_attention(qh, kh, vh, sink)
        new_kv = (kh, vh)
    else:
        kc, vc = ctx_kv
        o = banded_window_attention(qh, kh, vh, kc, vc, sink)
        new_kv = None
    yd = multiscale_pool(xd, pool_w, pool_scale)
    y = jnp.concatenate([merge_heads(o), yd], axis=-1) @ w_out
    return y, new_kv

def swiglu(h, w1, w3, w2):
    return (jax.nn.silu(h @ w1) * (h @ w3)) @ w2

def moe_swiglu(h, router_w, router_b, w1, w3, w2):
    b, s, d = h.shape
    t = h.reshape(b * s, d)
    logits = (t @ router_w).astype(jnp.float32) + router_b.astype(jnp.float32)
    top_v, top_i = lax.top_k(logits, TOP_K)
    gates = jax.nn.softmax(top_v, axis=-1)
    dense_g = jnp.sum(jax.nn.one_hot(top_i, N_EXPERTS, dtype=jnp.float32) * gates[..., None], axis=1)
    hid = jax.nn.silu(jnp.einsum('nd,edf->enf', t, w1)) * jnp.einsum('nd,edf->enf', t, w3)
    hid = hid * dense_g.T.astype(hid.dtype)[:, :, None]
    return jnp.einsum('enf,efd->nd', hid, w2).reshape(b, s, d)

def run_trunk(x, cond, cache_k, cache_v, rope, norm1, norm2, w_mod, b_mod,
              ev_w_in, ev_conv, ev_q_norm, ev_k_norm, ev_w_out,
              od_w_in, od_q_norm, od_k_norm, od_sink, od_pool_w, od_pool_scale, od_w_out,
              ffn_w1, ffn_w3, ffn_w2, moe_router, moe_router_b, moe_w1, moe_w3, moe_w2):
    ks, vs = [], []
    for l in range(DEPTH):
        i = l // 2
        sh1, sc1, g1, sh2, sc2, g2 = modulation(cond, w_mod[l], b_mod[l])
        h = rms_norm(x, norm1[l]) * (1.0 + sc1) + sh1
        ctx_kv = None if cache_k is None else (cache_k[:, l], cache_v[:, l])
        if l % 2 == 0:
            y, kv = even_mixer(h, ev_w_in[i], ev_conv[i], ev_q_norm[i], ev_k_norm[i], ev_w_out[i], ctx_kv, rope)
        else:
            y, kv = odd_mixer(h, od_w_in[i], od_q_norm[i], od_k_norm[i], od_sink[i],
                              od_pool_w[i], od_pool_scale[i], od_w_out[i], ctx_kv, rope)
        x = x + g1 * y
        h = rms_norm(x, norm2[l]) * (1.0 + sc2) + sh2
        if l % 2 == 0:
            f = swiglu(h, ffn_w1[i], ffn_w3[i], ffn_w2[i])
        else:
            f = moe_swiglu(h, moe_router[i], moe_router_b[i], moe_w1[i], moe_w3[i], moe_w2[i])
        x = x + g2 * f
        if kv is not None:
            ks.append(kv[0])
            vs.append(kv[1])
    return x, ks, vs

def setup_inputs(seed: int = 0) -> dict:
    key = jax.random.key(seed)
    keys = iter(jax.random.split(key, 40))

    def nrm(shape, scale):
        return jax.random.normal(next(keys), shape, jnp.float32) * scale

    def gain(shape):
        return 1.0 + nrm(shape, 0.05)

    kv_cache_shape = (DEC_BATCH, DEPTH, N_KV_HEADS, PAST_LEN, HEAD_DIM)
    return {
        'x_prompt': nrm((BATCH, SEQ, D_MODEL), 1.0),
        'x_sample': nrm((DEC_BATCH, DEC_SEQ, D_MODEL), 1.0),
        'cache_k': nrm(kv_cache_shape, 1.0),
        'cache_v': nrm(kv_cache_shape, 1.0),
        'c': nrm((DEC_BATCH, D_MODEL), 1.0),
        'c_ctx': nrm((D_MODEL,), 1.0),
        'norm1': gain((DEPTH, D_MODEL)),
        'norm2': gain((DEPTH, D_MODEL)),
        'w_mod': nrm((DEPTH, D_MODEL, 6 * D_MODEL), 0.5 * D_MODEL ** -0.5),
        'b_mod': nrm((DEPTH, 6 * D_MODEL), 0.02),
        'ev_w_in': nrm((N_EVEN, D_MODEL, EVEN_IN), D_MODEL ** -0.5),
        'ev_conv': nrm((N_EVEN, CONV_K, CONV_WIDTH), CONV_K ** -0.5),
        'ev_q_norm': gain((N_EVEN, HEAD_DIM)),
        'ev_k_norm': gain((N_EVEN, HEAD_DIM)),
        'ev_w_out': nrm((N_EVEN, MIX_WIDTH, D_MODEL), MIX_WIDTH ** -0.5),
        'od_w_in': nrm((N_ODD, D_MODEL, ODD_IN), D_MODEL ** -0.5),
        'od_q_norm': gain((N_ODD, HEAD_DIM)),
        'od_k_norm': gain((N_ODD, HEAD_DIM)),
        'od_sink': nrm((N_ODD, N_Q_HEADS), 0.5),
        'od_pool_w': nrm((N_ODD, len(POOL_WINDOWS), POOL_GROUP, POOL_GROUP), POOL_GROUP ** -0.5),
        'od_pool_scale': gain((N_ODD, POOL_WIDTH)),
        'od_w_out': nrm((N_ODD, MIX_WIDTH, D_MODEL), MIX_WIDTH ** -0.5),
        'ffn_w1': nrm((N_EVEN, D_MODEL, D_FF), D_MODEL ** -0.5),
        'ffn_w3': nrm((N_EVEN, D_MODEL, D_FF), D_MODEL ** -0.5),
        'ffn_w2': nrm((N_EVEN, D_FF, D_MODEL), D_FF ** -0.5),
        'moe_router': nrm((N_ODD, D_MODEL, N_EXPERTS), D_MODEL ** -0.5),
        'moe_router_b': nrm((N_ODD, N_EXPERTS), 0.01),
        'moe_w1': nrm((N_ODD, N_EXPERTS, D_MODEL, D_FF_EXPERT), D_MODEL ** -0.5),
        'moe_w3': nrm((N_ODD, N_EXPERTS, D_MODEL, D_FF_EXPERT), D_MODEL ** -0.5),
        'moe_w2': nrm((N_ODD, N_EXPERTS, D_FF_EXPERT, D_MODEL), D_FF_EXPERT ** -0.5),
    }

def reference(x_prompt, x_sample, cache_k, cache_v, c, c_ctx, norm1, norm2, w_mod, b_mod,
              ev_w_in, ev_conv, ev_q_norm, ev_k_norm, ev_w_out,
              od_w_in, od_q_norm, od_k_norm, od_sink, od_pool_w, od_pool_scale, od_w_out,
              ffn_w1, ffn_w3, ffn_w2, moe_router, moe_router_b, moe_w1, moe_w3, moe_w2):
    weights = (norm1, norm2, w_mod, b_mod,
               ev_w_in, ev_conv, ev_q_norm, ev_k_norm, ev_w_out,
               od_w_in, od_q_norm, od_k_norm, od_sink, od_pool_w, od_pool_scale, od_w_out,
               ffn_w1, ffn_w3, ffn_w2, moe_router, moe_router_b, moe_w1, moe_w3, moe_w2)
    y_prompt, ks, vs = run_trunk(x_prompt, c_ctx[None, :], None, None, None, *weights)
    new_k = jnp.stack(ks, axis=1)
    new_v = jnp.stack(vs, axis=1)
    rope = axial_rope_tables(x_sample.shape[1])
    y_sample, _, _ = run_trunk(x_sample, c, cache_k, cache_v, rope, *weights)
    return (y_prompt, y_sample, new_k, new_v)


_drawn_inputs = setup_inputs


def setup_inputs(seed=0):
    import zlib

    import numpy as np

    out = dict(_drawn_inputs(seed))
    spreads = {}
    factors = {'cache_k': 3.634,
     'cache_v': 2.874,
     'ev_q_norm': 8.0,
     'od_q_norm': 6.268,
     'od_sink': 52.952,
     'od_pool_scale': 4.426,
     'moe_router_b': 19.832}
    for name, (base, spread) in spreads.items():
        noise = np.random.default_rng([zlib.crc32(name.encode()), seed]).standard_normal(out[name].shape)
        drawn = base * np.exp(spread * noise) if base else spread * noise
        out[name] = __import__('jax').numpy.asarray(drawn.astype(out[name].dtype))
    for name, factor in factors.items():
        out[name] = (out[name] * factor).astype(out[name].dtype)
    return out
```

```python
from contextlib import ExitStack

import concourse.bass as bass
from concourse import mybir

F32 = mybir.dt.float32
F32R = mybir.dt.float32r
I32 = mybir.dt.int32
ALU = mybir.AluOpType
ACT = mybir.ActivationFunctionType
AX = mybir.AxisListType.X

P = 128
D = 1024
KT = D // P
LAT, CTX = 512, 128
TOK = LAT + CTX
TT = TOK // P
HALF = TOK // 2
PAST = 256
HD = 64
SCALE = HD ** -0.5
EPS = 1e-6
NMOD = 6 * D // P
SLAB = 256
NE = 8
CAP = 256
ROUNDS = -(-TOK // CAP)
NCAND = ROUNDS * NE
MAX_ITEMS = NE + 2 * TOK // (CAP + 1)
FFN_PARTS = (8, 8, 6)
PADW = 8 + LAT + 16 + CTX + 8
CTX0 = 8 + LAT + 16
NEG = -1e30

S_IN = (0, 47)
S_OUT = (9, 52)
S_FFN = 13
S_MOE = 56
S_LAST = 55
T_IN = (0, 134)
T_ATT = (18, 144)
T_OUT = (58, 184)
T_FFN = 66
T_TOK = 192
T_MOE = 202
ITEM_TILES = KT + 16 + 8 + KT
ITEM_SLABS = 12
M_NORM = (0, 47, 48, 99)
M_V = (1, 53)
M_POOL = 49
M_VAR = (2, 54)
M_ATT = (7, 59)
M_LOGIT, M_RANK, M_MOE = 100, 101, 102
O_ROT = (0, 45)
O_ATT = (5, 50)
P_CONV, P_FFN, P_MOE = 0, 4, 26

_KEPT = [("bmod", 2 * NMOD), ("norm1", 2 * KT), ("norm2", 2 * KT), ("cond", 2 * KT), ("conv", 12),
         ("pscale", 4), ("gain", 4), ("sink", 8), ("rbias", NE), ("edge", 64), ("ident", P), ("ones", P)]
_MIXER = [("kc", 2 * PAST), ("vc", 2 * PAST), ("poolw", 4 * P), ("rot", P), ("blk", P), ("mprev", P),
          ("mnext", P), ("cos", LAT), ("sin", LAT)]
_ROUTE = [("router", KT * NE), ("upper", P), ("desc", NE), ("thr", NCAND), ("cand", NCAND),
          ("u24", NCAND * NCAND), ("jidx", MAX_ITEMS * NCAND)]


def offsets(table):
    out, at = {}, 0
    for name, n in table:
        out[name] = (at, n)
        at += n
    return out, at


KEPT, NKEPT = offsets(_KEPT)
MIXER, NMIXER = offsets(_MIXER)
ROUTE, NROUTE = offsets(_ROUTE)


def attn_keys(layer, b):
    if b == TT - 1:
        return [("lat", LAT, CTX, None)]
    if layer == 0:
        return [("past", 0, PAST, None), ("lat", 0, 256, None), ("lat", 256, 256, None)]
    out = [("past", 0, PAST, None)]
    for o, mask in ((-1, "mprev"), (0, None), (1, "mnext")):
        if 0 <= b + o < LAT // P:
            out.append(("lat", (b + o) * P, P, mask))
    return out


def build(nc, xT_d, kept_d, mixer_d, route_d, iota_d, wmod_d, ws_d, y_d, newk_d, newv_d):
    with ExitStack() as ctx:
        def sb(name, shape, dt=F32, scope=ctx):
            return scope.enter_context(nc.sbuf_tensor(name, shape, dt))

        def sem(name):
            return ctx.enter_context(nc.semaphore(name))

        xT = sb("xT", [P, KT, TOK])
        raw = [sb(f"raw{i}", [P, 8, SLAB]) for i in range(2)]
        w_hi = [sb(f"w_hi{i}", [P, 8, SLAB], F32R) for i in range(2)]
        w_lo = [sb(f"w_lo{i}", [P, 8, SLAB], F32R) for i in range(2)]
        modraw = [sb(f"modraw{i}", [P, 8, P]) for i in range(4)]
        kept = sb("kept", [P, NKEPT])
        modv = sb("modv", [P, 2 * NMOD, 2])
        gainA = sb("gainA", [P, KT, 2])
        scond = sb("scond", [P, KT, 2])
        tmpA = sb("tmpA", [P, 2 * PADW])
        tmpB = sb("tmpB", [P, 2 * PADW])

        def kp(name, a=0, n=None):
            at, full = KEPT[name]
            return kept[:, at + a:at + (full if n is None else a + n)]

        def tA(c, n=TOK):
            return tmpA[:, c * PADW:c * PADW + n]

        def tB(c, n=TOK):
            return tmpB[:, c * PADW:c * PADW + n]

        with ExitStack() as r:
            h_hi = sb("h_hi", [P, KT, TOK], F32R, r)
            h_lo = sb("h_lo", [P, KT, TOK], F32R, r)
            with ExitStack() as r2:
                mix_hi = sb("mix_hi", [P, KT, TOK], F32R, r2)
                mix_lo = sb("mix_lo", [P, KT, TOK], F32R, r2)
                q = sb("q", [P, 4, TOK], F32, r2)
                k = sb("k", [P, TOK], F32, r2)
                v = sb("v", [P, TOK], F32, r2)
                v_tok = sb("v_tok", [P, TT, P], F32, r2)
            with ExitStack() as r2:
                fh_hi = sb("fh_hi", [P, 8, TOK], F32R, r2)
                fh_lo = sb("fh_lo", [P, 8, TOK], F32R, r2)
            with ExitStack() as r2:
                tok_hi = sb("tok_hi", [P, TT, D], F32R, r2)
                tok_lo = sb("tok_lo", [P, TT, D], F32R, r2)
                with ExitStack() as r3:
                    y_hi = sb("y_hi", [P, 2, D], F32R, r3)
                    y_lo = sb("y_lo", [P, 2, D], F32R, r3)
                route = sb("route", [P, NROUTE], F32, r2)
                rw_hi = sb("rw_hi", [P, KT * NE], F32R, r2)
                rw_lo = sb("rw_lo", [P, KT * NE], F32R, r2)
                rt = sb("rt", [P, 12, TT * NE], F32, r2)
                rc = sb("rc", [P, 6, NCAND], F32, r2)
                rsel = sb("rsel", [P, MAX_ITEMS, NCAND], F32, r2)
                rbig = sb("rbig", [P, TT * MAX_ITEMS * NCAND], F32, r2)
                rcand = sb("rcand", [P, TT, NCAND], F32, r2)
        with ExitStack() as r:
            probs = [sb(f"probs{i}", [P, 6 * P], F32, r) for i in range(2)]
            probsT = [sb(f"probsT{i}", [P, 6, P], F32, r) for i in range(2)]
            qcur = sb("qcur", [P, TOK], F32, r)
        with ExitStack() as r:
            g_hl = sb("g_hl", [P, KT, 2, CAP], F32R, r)
            e_hi = sb("e_hi", [P, 8, CAP], F32R, r)
            e_lo = sb("e_lo", [P, 8, CAP], F32R, r)
        sb("region1", [P, 2 * KT * TOK])
        sb("region2", [P, 2 * KT * TOK + 4 * TOK + 3 * TOK])

        with ExitStack() as r:
            mixer = sb("mixer", [P, NMIXER], F32, r)
        iota = sb("iota", [P, CAP])
        onehot = sb("onehot", [P, TT, CAP], F32R)
        selT = sb("selT", [P, 2, TOK], F32R)
        sb("region3_rest", [P, NMIXER - CAP - TT * CAP - 2 * TOK])

        def mx(name, a=0, n=None):
            at, full = MIXER[name]
            return mixer[:, at + a:at + (full if n is None else a + n)]

        def ro(name, a=0, n=None):
            at, full = ROUTE[name]
            return route[:, at + a:at + (full if n is None else a + n)]

        ident, ones = kp("ident"), kp("ones")
        soft = sb("soft", [P, 2, 5])
        item_pos = sb("item_pos", [P, TT, MAX_ITEMS])
        item_gate = sb("item_gate", [P, TT, MAX_ITEMS])
        item_no = sb("item_no", [P, MAX_ITEMS + 1], I32)
        gslot = sb("gslot", [P, 2])
        nsink = sb("nsink", [P, 8])
        sinkcur = sb("sinkcur", [P, 2])
        eps = sb("eps", [P, 1])

        pp = [ctx.enter_context(nc.psum_tensor(f"pp{i}", [P, 1024], F32)) for i in range(2)]
        pm = ctx.enter_context(nc.psum_tensor("pm", [P, 1024], F32))
        po = ctx.enter_context(nc.psum_tensor("po", [P, 512], F32))
        pmod = ctx.enter_context(nc.psum_tensor("pmod", [P, 512], F32))

        kept_in, x_in, mixer_in, route_in, iota_in = (sem(n) for n in ("kept_in", "x_in", "mixer_in", "route_in", "iota_in"))
        slab_in = [sem(f"slab_in{i}") for i in range(2)]
        mod_in = [sem(f"mod_in{i}") for i in range(4)]
        w_hi_done, w_lo_done = sem("w_hi_done"), sem("w_lo_done")
        cond_ready, mod_used, mod_kept = sem("cond_ready"), sem("mod_used"), sem("mod_kept")
        tile_done = sem("tile_done")
        tile_free = [sem(f"tile_free{i}") for i in range(2)]
        pm_done, pm_free, po_done, po_free = sem("pm_done"), sem("pm_free"), sem("po_done"), sem("po_free")
        sq_ready, sq_used, scaled, h_hi_done, h_ready = (sem(n) for n in ("sq_ready", "sq_used", "scaled", "h_hi_done", "h_ready"))
        prod_hi, prod_lo = sem("prod_hi"), sem("prod_lo")
        zsq_ready, zn_ready, rotated, qk_ready = sem("zsq_ready"), sem("zn_ready"), sem("rotated"), sem("qk_ready")
        pooled, pool_hi, pads_zero = sem("pooled"), sem("pool_hi"), sem("pads_zero")
        q_ready, rowmax_done, negmax_done, den_done, rsum_done, p_ready, o_hi_done = (
            sem(n) for n in ("q_ready", "rowmax_done", "negmax_done", "den_done", "rsum_done", "p_ready", "o_hi_done"))
        kv_out, y_out = sem("kv_out"), sem("y_out")
        rw_hi_done, rw_ready, gap_ready, gap_exp, mask_ready, routed = (
            sem(n) for n in ("rw_hi_done", "rw_ready", "gap_ready", "gap_exp", "mask_ready", "routed"))
        eps_set = sem("eps_set")
        onehot_ready, yhi_done, dve_step = sem("onehot_ready"), sem("yhi_done"), sem("dve_step")

        block = ctx.enter_context(nc.Block())

        def two(a):
            return a.rearrange("p (h n) -> p h n", h=2)

        def banks(pair):
            return pair[:].rearrange("p (h n) -> p h n", h=2)[:, :, 0:HALF]

        pieces = ((0, HALF, 0), (HALF, LAT, 0), (LAT, TOK, 1))

        def at_bank(a, b):
            return slice(a, b) if b <= HALF else slice(512 + a - HALF, 512 + b - HALF)

        def tiles_after(s):
            for s0, t0 in ((S_OUT[1], T_OUT[1]), (S_IN[1], T_IN[1]), (S_FFN, T_FFN), (S_OUT[0], T_OUT[0]), (0, 0)):
                if s >= s0:
                    return t0 + 2 * (s - s0) + 2

        def half(n, it=0, step=0):
            return n // 2 + it * (step // 2)

        def taken(eng, t, it=0, step=0):
            eng.wait_ge(tile_free[t % 2], half(t, it, step) + 1)

        def items(eng):
            eng.wait_ge(routed, 1)
            return eng.value_load(item_no[0:1, MAX_ITEMS:MAX_ITEMS + 1], min_val=NE, max_val=MAX_ITEMS)

        @block.sync
        def _(sp):
            sp.dma_start(kept[:], kept_d).then_inc(kept_in, 16)
            for c in range(2):
                sp.dma_start(raw[c][:], ws_d[c].rearrange("p (k n) -> p k n", k=8)).then_inc(slab_in[c], 16)
            sp.dma_start(xT[:], xT_d).then_inc(x_in, 16)
            sp.dma_start(mixer[:], mixer_d).then_inc(mixer_in, 16)
            with sp.Fori(1, (S_MOE + ITEM_SLABS * NE) // 2) as i:
                for c in range(2):
                    sp.wait_ge(w_lo_done, i * 2 + (c - 1))
                    sp.dma_start(raw[c][:], ws_d[bass.ds(i * 2 + c, 1)].rearrange("a p (k n) -> (a p) k n", k=8)
                                 ).then_inc(slab_in[c], 16)
            n_items = items(sp)
            with sp.If(n_items > NE):
                with sp.Fori(NE, n_items) as j:
                    e = sp.value_load(item_no[0:1, bass.ds(j, 1)], min_val=0, max_val=NE - 1)
                    for c2 in range(ITEM_SLABS // 2):
                        for c in range(2):
                            sp.wait_ge(w_lo_done, j * ITEM_SLABS + (S_MOE + 2 * c2 + c - 1))
                            sp.dma_start(raw[c][:], ws_d[bass.ds(e * ITEM_SLABS + (S_MOE + 2 * c2 + c), 1)].rearrange(
                                "a p (k n) -> (a p) k n", k=8)).then_inc(slab_in[c], 16)
            for c in range(2):
                sp.wait_ge(tile_free[c], n_items * (ITEM_TILES // 2) + T_MOE // 2)
            sp.dma_start(y_d, xT[:]).then_inc(y_out, 16)
            sp.wait_ge(y_out, 16)
            sp.wait_ge(kv_out, 64)

        @block.gpsimd
        def _(pool):
            for c in range(4):
                pool.dma_start(modraw[c][:], wmod_d[c].rearrange("p (k n) -> p k n", k=8)).then_inc(mod_in[c], 16)
            with pool.Fori(1, 2 * NMOD // 4) as i:
                for c in range(4):
                    pool.wait_ge(mod_used, i * 4 + (c - 3))
                    pool.dma_start(modraw[c][:], wmod_d[bass.ds(i * 4 + c, 1)].rearrange("a p (k n) -> (a p) k n", k=8)
                                   ).then_inc(mod_in[c], 16)
            pool.wait_ge(tile_done, T_OUT[1] + 8)
            pool.dma_start(route[:], route_d).then_inc(route_in, 16)
            pool.dma_start(iota[:], iota_d).then_inc(iota_in, 16)

        @block.tensor
        def _(pe):
            mm = nc.tensor.matmul

            def mods(n0, count, it=0, step=0):
                for c in range(count):
                    n = n0 + c
                    pe.wait_ge(mod_in[n % 4], 16 * (n // 4 + 1) + it * (16 * step // 4))
                    col = it * (2 * step) + 2 * (n % NMOD)
                    for kt in range(KT):
                        last = mm(pmod[:, bass.ds(col, 2)], modraw[n % 4][:, kt, :], scond[:, kt, :],
                                  start=kt == 0, stop=kt == KT - 1)
                    last.then_inc(mod_used, 1)

            def mod_group(g):
                if g:
                    pe.wait_ge(mod_kept, g)
                    with pe.Fori(0, 4) as i:
                        mods(16 * g, 4, it=i, step=4)
                else:
                    mods(0, 4)
                    with pe.Fori(1, 4) as i:
                        mods(0, 4, it=i, step=4)

            def tile_slot(t, it, step):
                if t >= 2 or step:
                    pe.wait_ge(tile_free[t % 2], half(t, it, step))
                return pp[t % 2]

            def three(out, a_hi, a_lo, b_hi, b_lo, first, last, n):
                for x, y, f in ((a_hi, b_hi, first), (a_hi, b_lo, False), (a_lo, b_hi, False)):
                    end = last and x is a_lo
                    for lo, hi in ((0, HALF), (HALF, TOK)) if n == TOK else ((0, n),):
                        ins = mm(out[:, at_bank(lo, hi)], x, y[:, lo:hi], start=f, stop=end)
                return ins

            def slab(s, t, b_hi, b_lo, n=TOK, kk=KT, it=0, sstep=0, tstep=0, ready=None):
                if ready is not None:
                    outs = [tile_slot(t + c, it, tstep) for c in range(2)]
                    pe.wait_ge(w_lo_done, s + 1)
                    for kt in range(kk):
                        pe.wait_ge(h_ready, ready + kt + 1)
                        for c in range(2):
                            w = (slice(None), kt, slice(c * P, c * P + P))
                            ins = three(outs[c], w_hi[s % 2][w], w_lo[s % 2][w], b_hi[:, kt], b_lo[:, kt], kt == 0, kt == kk - 1, n)
                            if kt == kk - 1:
                                ins.then_inc(tile_done, 1)
                    return
                for c in range(2):
                    out = tile_slot(t + c, it, tstep)
                    if c == 0:
                        pe.wait_ge(w_hi_done, it * sstep + (s + 1))
                        pe.wait_ge(w_lo_done, it * sstep + (s + 1))
                    for kt in range(kk):
                        w = (slice(None), kt, slice(c * P, c * P + P))
                        ins = three(out, w_hi[s % 2][w], w_lo[s % 2][w], b_hi[:, kt], b_lo[:, kt], kt == 0, kt == kk - 1, n)
                    ins.then_inc(tile_done, 1)

            def use_pm(m):
                if not (isinstance(m, int) and m == 0):
                    pe.wait_ge(pm_free, m)

            def norm(n):
                use_pm(M_NORM[n])
                for kt in range(KT):
                    pe.wait_ge(sq_ready, KT * n + kt + 1)
                    for lo, hi in ((0, HALF), (HALF, TOK)):
                        last = mm(pm[:, at_bank(lo, hi)], ones, tA(kt % 2)[:, lo:hi], start=kt == 0, stop=kt == KT - 1)
                    last.then_inc(sq_used if kt < KT - 1 else pm_done, 1)

            def project_in(l):
                s, t = S_IN[l], T_IN[l]
                slab(s, t, h_hi, h_lo, ready=KT * 2 * l)
                with pe.Fori(0, (4, 2)[l]) as i:
                    for c in range(2):
                        slab(s + 1 + c, t + 2 + 2 * c, h_hi, h_lo, it=i, sstep=2, tstep=4)

            def qk_norm(l):
                if l == 0:
                    pe.wait_ge(mixer_in, 16)
                if l == 1:
                    for g in range(4):
                        pe.wait_ge(pooled, g + 1)
                        use_pm(M_POOL + g)
                        for a, b, x in pieces:
                            at = a + (8 if x == 0 else CTX0 - LAT)
                            last = mm(pm[:, at_bank(a, b)], mx("poolw", g * P, P), tB((g + 1) % 2, PADW)[:, at:at + b - a],
                                      start=True, stop=True)
                        last.then_inc(pm_done, 1)
                for t in (4, 5):
                    taken(pe, T_IN[l] + t)
                use_pm(M_V[l])
                for t in range(TT):
                    last = nc.tensor.transpose(pm[:, t * P:(t + 1) * P], v[:, t * P:(t + 1) * P], ident)
                last.then_inc(pm_done, 1)
                mod_group((2, 5)[l])
                for j in range(5):
                    pe.wait_ge(zsq_ready, 5 * l + j + 1)
                    use_pm(M_VAR[l] + j)
                    for lo, hi in ((0, HALF), (HALF, TOK)):
                        last = mm(pm[:, at_bank(lo, hi)], mx("blk"), tA(j % 2)[:, lo:hi], start=True, stop=True)
                    last.then_inc(pm_done, 1)
                    pe.wait_ge(zn_ready, 5 * l + j + 1)
                    if O_ROT[l] + j:
                        pe.wait_ge(po_free, O_ROT[l] + j)
                    z = q[:, j] if j < 4 else k[:]
                    mm(po[:], mx("rot"), z[:, 0:LAT], start=True, stop=True).then_inc(po_done, 1)

            def attention(l):
                pe.wait_ge(qk_ready, l + 1)
                def scores(c, i):
                    g, b = divmod(c, TT)
                    out = tile_slot(T_ATT[l] + c, i, 10)
                    at, rows = 0, slice(g * HD, g * HD + HD)
                    for src, k0, n, mask in attn_keys(l, b):
                        keys = mx("kc", l * PAST, PAST)[rows] if src == "past" else k[rows, k0:k0 + n]
                        last = mm(out[:, at:at + n], qcur[rows, b * P:(b + 1) * P], keys, start=True, stop=mask is None)
                        if mask:
                            last = mm(out[:, at:at + n], ident, mx(mask), start=False, stop=True)
                        at += n
                    last.then_inc(tile_done, 1)

                def turn(c, i):
                    n = sum(x[2] for x in attn_keys(l, c % TT)) // P
                    pe.wait_ge(p_ready, i * 10 + (40 * l + c + 1))
                    use_pm(i * 10 + (M_ATT[l] + c))
                    for kt in range(n):
                        last = nc.tensor.transpose(pm[:, kt * P:(kt + 1) * P], probs[c % 2][:, kt * P:(kt + 1) * P], ident)
                    last.then_inc(pm_done, 1)

                def values(c, i):
                    pe.wait_ge(pm_free, i * 10 + (M_ATT[l] + c + 1))
                    pe.wait_ge(po_free, i * 10 + (O_ATT[l] + c))
                    vs = []
                    for src, k0, n, _ in attn_keys(l, c % TT):
                        for kt in range(n // P):
                            vs.append(mx("vc", l * PAST + kt * P, P) if src == "past" else v_tok[:, k0 // P + kt])
                    for kt, vt in enumerate(vs):
                        last = mm(po[:, 0:P], vt, probsT[c % 2][:, kt], start=kt == 0, stop=kt == len(vs) - 1)
                    last.then_inc(po_done, 1)

                with pe.Fori(0, 4) as i:
                    pe.wait_ge(q_ready, i + (4 * l + 1))
                    scores(0, i)
                    for c in range(10):
                        if c < 9:
                            scores(c + 1, i)
                        turn(c, i)
                        if c:
                            values(c - 1, i)
                    values(9, i)

            def project_out(l):
                pe.wait_ge(po_free, O_ATT[l] + 40)
                if l == 0:
                    pe.wait_ge(prod_lo, P_FFN)
                else:
                    pe.wait_ge(pm_free, M_NORM[3])
                with pe.Fori(0, 2) as i:
                    for c in range(2):
                        slab(S_OUT[l] + c, T_OUT[l] + 2 * c, mix_hi, mix_lo, it=i, sstep=2, tstep=4)

            def ffn():
                s, t, p = S_FFN, T_FFN, P_FFN
                for n, hidden in enumerate(FFN_PARTS):
                    if n == 0:
                        slab(s, t, h_hi, h_lo, ready=KT)
                        slab(s + 1, t + 2, h_hi, h_lo)
                    with pe.Fori(int(n == 0), hidden // 2) as i:
                        for c in range(2):
                            slab(s + c, t + 2 * c, h_hi, h_lo, it=i, sstep=2, tstep=4)
                    s, t, p = s + hidden, t + 2 * hidden, p + hidden
                    pe.wait_ge(prod_lo, p)
                    with pe.Fori(0, 2) as i:
                        for c in range(2):
                            slab(s + c, t + 2 * c, fh_hi, fh_lo, kk=hidden, it=i, sstep=2, tstep=4)
                    s, t = s + 4, t + 8

            def routing():
                pe.wait_ge(h_ready, 4 * KT)
                pe.wait_ge(rw_ready, 1)
                use_pm(M_LOGIT)
                for t in range(TT):
                    for kt in range(KT):
                        a = (slice(None), kt, slice(t * P, t * P + P))
                        r = slice(kt * NE, kt * NE + NE)
                        last = three(pm[:, t * NE:(t + 1) * NE], h_hi[a], h_lo[a], rw_hi[:, r], rw_lo[:, r], kt == 0, kt == KT - 1, NE)
                last.then_inc(pm_done, 1)
                for n in range(2 * TT):
                    out = tile_slot(T_TOK + n, 0, 0)
                    src = h_hi if n < TT else h_lo
                    t = n % TT
                    for kt in range(KT):
                        last = nc.tensor.transpose(out[:, kt * P:(kt + 1) * P], src[:, kt, t * P:(t + 1) * P].bitcast(F32), ident)
                    last.then_inc(tile_done, 1)
                pe.wait_ge(mask_ready, 1)
                use_pm(M_RANK)
                mask = rt[:, 11, :]
                for t in range(TT):
                    for u in range(t + 1):
                        mm(pm[:, t * NE:(t + 1) * NE], ro("upper") if u == t else ones, mask[:, u * NE:(u + 1) * NE],
                           start=u == 0, stop=u == t)
                for t in range(TT):
                    last = mm(pm[:, TT * NE:(TT + 1) * NE], ones, mask[:, t * NE:(t + 1) * NE], start=t == 0, stop=t == TT - 1)
                last.then_inc(pm_done, 1)

            def experts():
                n_items = items(pe)
                for t in (2, 1):
                    taken(pe, T_MOE - t)
                with pe.Fori(0, n_items) as j:
                    pe.wait_ge(onehot_ready, j + 1)
                    use_pm(j * 3 + M_MOE)
                    for sl in range(2):
                        for t in range(TT):
                            last = mm(pm[:, sl:sl + 1], onehot[:, t, sl * P:(sl + 1) * P].bitcast(F32),
                                      item_gate[:, t, bass.ds(j, 1)], start=t == 0, stop=t == TT - 1)
                    last.then_inc(pm_done, 1)
                    for sl in range(2):
                        use_pm(j * 3 + (M_MOE + 1 + sl))
                        for t in range(TT):
                            last = nc.tensor.transpose(pm[:, t * P:(t + 1) * P], onehot[:, t, sl * P:(sl + 1) * P].bitcast(F32), ident)
                        last.then_inc(pm_done, 1)
                    T = T_MOE
                    for kt in range(KT):
                        out = tile_slot(T + kt, j, ITEM_TILES)
                        for x, src in enumerate((tok_hi, tok_lo)):
                            for t in range(TT):
                                last = mm(out[:, x * CAP:(x + 1) * CAP], src[:, t, kt * P:(kt + 1) * P], onehot[:, t, :],
                                          start=t == 0, stop=t == TT - 1)
                        last.then_inc(tile_done, 1)
                    T += KT
                    with pe.Fori(0, 4) as i:
                        pe.wait_ge(tile_free[0], j * (ITEM_TILES // 2) + T // 2)
                        pe.wait_ge(tile_free[1], j * (ITEM_TILES // 2) + T // 2)
                        for w in range(2):
                            for c in range(2):
                                t = T + 2 * w + c
                                pe.wait_ge(tile_free[t % 2], j * (ITEM_TILES // 2) + i * 2 + t // 2)
                                if c == 0:
                                    pe.wait_ge(w_hi_done, j * ITEM_SLABS + i * 2 + (S_MOE + w + 1))
                                    pe.wait_ge(w_lo_done, j * ITEM_SLABS + i * 2 + (S_MOE + w + 1))
                                for kt in range(KT):
                                    a = (slice(None), kt, slice(c * P, c * P + P))
                                    last = three(pp[t % 2], w_hi[w][a], w_lo[w][a], g_hl[:, kt, 0], g_hl[:, kt, 1], kt == 0, kt == KT - 1, CAP)
                                last.then_inc(tile_done, 1)
                    T += 16
                    pe.wait_ge(prod_lo, j * 8 + (P_MOE + 8))
                    for n in range(4):
                        for sl in range(2):
                            out = tile_slot(T + 2 * n + sl, j, ITEM_TILES)
                            if sl == 0:
                                pe.wait_ge(w_hi_done, j * ITEM_SLABS + (S_MOE + 8 + n + 1))
                                pe.wait_ge(w_lo_done, j * ITEM_SLABS + (S_MOE + 8 + n + 1))
                            for f in range(8):
                                a = (slice(None), f, slice(sl * P, sl * P + P))
                                last = three(out, e_hi[a], e_lo[a], w_hi[n % 2][:, f], w_lo[n % 2][:, f], f == 0, f == 7, SLAB)
                            last.then_inc(tile_done, 1)
                    T += 8
                    pe.wait_ge(tile_free[0], j * (ITEM_TILES // 2) + T // 2)
                    pe.wait_ge(tile_free[1], j * (ITEM_TILES // 2) + T // 2)
                    pe.wait_ge(pm_free, j * 3 + (M_MOE + 3))
                    for d in range(KT):
                        out = tile_slot(T + d, j, ITEM_TILES)
                        for sl in range(2):
                            for y in (y_hi, y_lo):
                                for lo, hi in ((0, HALF), (HALF, TOK)):
                                    last = mm(out[:, at_bank(lo, hi)], y[:, sl, d * P:(d + 1) * P], selT[:, sl, lo:hi],
                                              start=sl == 0 and y is y_hi, stop=sl == 1 and y is y_lo)
                        last.then_inc(tile_done, 1)

            pe.wait_ge(cond_ready, 1)
            mod_group(0)
            norm(0)
            mod_group(1)
            project_in(0)
            qk_norm(0)
            attention(0)
            project_out(0)
            norm(1)
            mod_group(3)
            ffn()
            norm(2)
            mod_group(4)
            project_in(1)
            qk_norm(1)
            attention(1)
            project_out(1)
            norm(3)
            routing()
            experts()

        @block.scalar
        def _(act):
            A = nc.scalar.activation

            def hi(s, it=0, step=0, tstep=0):
                act.wait_ge(slab_in[s % 2], half(s, it, step) * 16 + 16)
                if s >= 2:
                    act.wait_ge(tile_done, it * tstep + tiles_after(s - 2))
                A(w_hi[s % 2][:], raw[s % 2][:], ACT.Copy).then_inc(w_hi_done, 1)

            def norm(n):
                l, second = divmod(n, 2)
                if n == 0:
                    act.wait_ge(x_in, 16)
                for kt in range(KT):
                    if n:
                        taken(act, (T_OUT[0], T_IN[1] - KT, T_OUT[1])[n - 1] + kt)
                    if kt >= 2:
                        act.wait_ge(sq_used, (KT - 1) * n + kt - 1)
                    A(tA(kt % 2), xT[:, kt], ACT.Square, scale=D ** -0.5).then_inc(sq_ready, 1)
                act.wait_ge(pm_done, M_NORM[n] + 1)
                A(two(tB(0)), banks(pm), ACT.Sqrt, bias=eps[:]).then_inc(pm_free, 1)
                for kt in range(KT):
                    act.wait_ge(scaled, KT * n + kt + 1)
                    for x, (a, b) in enumerate(((0, LAT), (LAT, TOK))):
                        last = A(h_hi[:, kt, a:b], tA(kt % 2)[:, a:b], ACT.Identity, bias=modv[:, NMOD * l + 24 * second + kt, x:x + 1])
                    last.then_inc(h_hi_done, 1)

            def copy_tile(t, dst):
                act.wait_ge(tile_done, t + 1)
                A(two(dst), banks(pp[t % 2]), ACT.Copy).then_inc(tile_free[t % 2], 1)

            def project_in(l):
                s, t = S_IN[l], T_IN[l]
                for n in range(3):
                    hi(s + 1)
                    for c in range(2):
                        j = 2 * n + c
                        copy_tile(t + c, q[:, j] if j < 4 else (k, v)[j - 4][:])
                    s, t = s + 1, t + 2
                if l == 0:
                    for n in range(2):
                        hi(s + 1)
                        for c in range(2):
                            copy_tile(t + c, tA(c))
                        hi(s + 2)
                        hi(s + 3)
                        for c in range(2):
                            taken(act, t + 4 + c)
                            A(mix_hi[:, 4 + 2 * n + c], tB(c), ACT.Copy).then_inc(prod_hi, 1)
                        s, t = s + 3, t + 6
                else:
                    act.wait_ge(pads_zero, 2)
                    for n in range(2):
                        hi(s + 1)
                        for c in range(2):
                            g = 2 * n + c
                            if g >= 2:
                                act.wait_ge(pooled, g - 1)
                            act.wait_ge(tile_done, t + c + 1)
                            for a, b, x in pieces:
                                at = a + (8 if x == 0 else CTX0 - LAT)
                                ins = A(tA(c, PADW)[:, at:at + b - a], pp[(t + c) % 2][:, at_bank(a, b)], ACT.Copy)
                            ins.then_inc(tile_free[(t + c) % 2], 1)
                        s, t = s + 1, t + 2

            def qk_norm(l):
                if l == 1:
                    for g in range(4):
                        act.wait_ge(pm_done, M_POOL + g + 1)
                        A(two(mix_hi[:, 4 + g]), banks(pm), ACT.Copy, scale=kp("pscale", g, 1)).then_inc(pool_hi, 1)
                act.wait_ge(pm_done, M_V[l] + 1)
                A(v_tok[:].rearrange("p t n -> p (t n)"), pm[:, 0:TOK], ACT.Copy).then_inc(pm_free, 1)
                def square(j):
                    A(tA(j % 2), q[:, j] if j < 4 else k[:], ACT.Square, scale=HD ** -0.5).then_inc(zsq_ready, 1)

                act.wait_ge(*((prod_lo, P_FFN), (pooled, 4))[l])
                square(0)
                for j in range(5):
                    if j < 4:
                        square(j + 1)
                    act.wait_ge(pm_done, M_VAR[l] + j + 1)
                    if j >= 2:
                        act.wait_ge(zn_ready, 5 * l + j)
                        act.wait_ge(rotated, 5 * l + j - 1)
                    A(two(tB(j % 2)), banks(pm), ACT.Sqrt, bias=eps[:]).then_inc(pm_free, 1)
                act.wait_ge(qk_ready, l + 1)
                act.dma_start(newk_d[l], k[:, LAT:TOK]).then_inc(kv_out, 16)
                act.dma_start(newv_d[l], v[:, LAT:TOK]).then_inc(kv_out, 16)

            def attention(l):
                def exps(c, i):
                    g, b = divmod(c, TT)
                    n = sum(x[2] for x in attn_keys(l, b))
                    act.wait_ge(negmax_done, i * 10 + (40 * l + c + 1))
                    if l == 1:
                        A(soft[:, c % 2, 4:5], sinkcur[:, g:g + 1], ACT.Exp, bias=soft[:, c % 2, 1:2])
                    ins = A(probs[c % 2][:, 0:n], pp[(T_ATT[l] + c) % 2][:, 0:n], ACT.Exp, bias=soft[:, c % 2, 1:2],
                            scale=SCALE, accum_out=soft[:, c % 2, 2:3])
                    ins.then_inc(tile_free[(T_ATT[l] + c) % 2], 1)

                def turned(c, i):
                    n = sum(x[2] for x in attn_keys(l, c % TT))
                    act.wait_ge(pm_done, i * 10 + (M_ATT[l] + c + 1))
                    A(probsT[c % 2][:, 0:n // P], pm[:, 0:n].rearrange("p (t n) -> p t n", n=P), ACT.Copy).then_inc(pm_free, 1)

                def out_hi(c, i):
                    g, b = divmod(c, TT)
                    rows = slice(g * HD, g * HD + HD)
                    act.wait_ge(po_done, i * 10 + (O_ATT[l] + c + 1))
                    A(mix_hi[rows, bass.ds(i, 1), b * P:(b + 1) * P], po[rows, 0:P].unsqueeze(1), ACT.Copy).then_inc(o_hi_done, 1)

                with act.Fori(0, 4) as i:
                    exps(0, i)
                    for c in range(10):
                        if c < 9:
                            exps(c + 1, i)
                        turned(c, i)
                        if c:
                            out_hi(c - 1, i)
                    out_hi(9, i)

            def ffn():
                act.wait_ge(kv_out, 32)
                s, t, p = S_FFN, T_FFN, P_FFN
                for hidden in FFN_PARTS:
                    hi(s + 1)
                    with act.Fori(0, hidden // 2) as i:
                        for c in range(2):
                            act.wait_ge(tile_done, i * 4 + (t + c + 1))
                            A(two(tA(c)), banks(pp[(t + c) % 2]), ACT.Silu).then_inc(tile_free[(t + c) % 2], 1)
                        hi(s + 2, i, 2, 4)
                        for c in range(2):
                            taken(act, t + 2 + c, i, 4)
                            A(fh_hi[:, bass.ds(i * 2 + c, 1)], tB(c).unsqueeze(1), ACT.Copy).then_inc(prod_hi, 1)
                        hi(s + 3, i, 2, 4)
                    s, t, p = s + hidden, t + 2 * hidden, p + hidden
                    for n in range(1, 4):
                        hi(s + n + 1)
                    s, t = s + 4, t + 8

            def routing():
                act.wait_ge(route_in, 16)
                A(rw_hi[:], ro("router"), ACT.Copy).then_inc(rw_hi_done, 1)
                act.wait_ge(kv_out, 64)
                for n in range(0, 2 * TT, 2):
                    act.wait_ge(tile_done, T_TOK + n + 1)
                    dst = (tok_hi if n < TT else tok_lo)[:, n % TT]
                    A(dst, pp[n % 2][:, :], ACT.Copy).then_inc(tile_free[n % 2], 1)
                act.wait_ge(gap_ready, 1)
                A(rc[:, 5, 0:TT], rc[:, 4, 0:TT], ACT.Exp).then_inc(gap_exp, 1)

            def experts():
                n_items = items(act)
                with act.Fori(0, n_items) as j:
                    act.wait_ge(slab_in[0], j * (8 * ITEM_SLABS) + (8 * S_MOE + 16))
                    act.wait_ge(tile_done, j * ITEM_TILES + (T_MOE - KT - 2))
                    A(w_hi[0][:], raw[0][:], ACT.Copy).then_inc(w_hi_done, 1)
                    act.wait_ge(pm_done, j * 3 + (M_MOE + 1))
                    A(gslot[:], pm[:, 0:2], ACT.Copy).then_inc(pm_free, 1)
                    for sl in range(2):
                        act.wait_ge(pm_done, j * 3 + (M_MOE + 2 + sl))
                        A(selT[:, sl], pm[:, 0:TOK], ACT.Copy).then_inc(pm_free, 1)
                    t = T_MOE + KT
                    with act.Fori(0, 4) as i:
                        act.wait_ge(slab_in[1], j * (8 * ITEM_SLABS) + i * 16 + (8 * S_MOE + 16))
                        act.wait_ge(tile_done, j * ITEM_TILES + i * 4 + t)
                        A(w_hi[1][:], raw[1][:], ACT.Copy).then_inc(w_hi_done, 1)
                        for c in range(2):
                            act.wait_ge(tile_done, j * ITEM_TILES + i * 4 + (t + c + 1))
                            A(tA(c, CAP), pp[(t + c) % 2][:, 0:CAP], ACT.Silu).then_inc(tile_free[(t + c) % 2], 1)
                        act.wait_ge(slab_in[0], j * (8 * ITEM_SLABS) + i * 16 + (8 * S_MOE + 32))
                        act.wait_ge(tile_done, j * ITEM_TILES + i * 4 + (t + 2))
                        A(w_hi[0][:], raw[0][:], ACT.Copy).then_inc(w_hi_done, 1)
                        for c in range(2):
                            act.wait_ge(tile_free[c], j * (ITEM_TILES // 2) + i * 2 + ((t + 2) // 2 + 1))
                            A(e_hi[:, bass.ds(i * 2 + c, 1)], tB(c, CAP).unsqueeze(1), ACT.Copy).then_inc(prod_hi, 1)
                    t += 16
                    for n in range(4):
                        if n < 3:
                            c = (n + 1) % 2
                            act.wait_ge(slab_in[c], j * (8 * ITEM_SLABS) + 16 * ((S_MOE + 9 + n) // 2 + 1))
                            act.wait_ge(tile_done, j * ITEM_TILES + (t + 2 * n))
                            A(w_hi[c][:], raw[c][:], ACT.Copy).then_inc(w_hi_done, 1)
                        for sl in range(2):
                            act.wait_ge(tile_done, j * ITEM_TILES + (t + 2 * n + sl + 1))
                            A(y_hi[:, sl, n * SLAB:(n + 1) * SLAB], pp[sl][:, 0:SLAB], ACT.Copy, scale=gslot[:, sl:sl + 1]
                              ).then_inc(yhi_done, 1)

            act.wait_ge(eps_set, 1)
            act.wait_ge(kept_in, 16)
            A(scond[:].rearrange("p k c -> p (k c)"), kp("cond"), ACT.Silu).then_inc(cond_ready, 1)
            hi(0)
            norm(0)
            project_in(0)
            qk_norm(0)
            attention(0)
            for n in range(4):
                hi(S_OUT[0] + n + 1)
            norm(1)
            ffn()
            norm(2)
            project_in(1)
            qk_norm(1)
            attention(1)
            for n in range(3):
                hi(S_OUT[1] + n + 1)
            norm(3)
            routing()
            experts()

        @block.vector
        def _(dve):
            V = nc.vector
            steps = [0]

            def step(ins):
                steps[0] += 1
                ins.then_inc(dve_step, 1)
                dve.wait_ge(dve_step, steps[0])

            def lo(s, it=0, sstep=0):
                dve.wait_ge(w_hi_done, it * sstep + (s + 1))
                V.tensor_tensor(w_lo[s % 2][:], raw[s % 2][:], w_hi[s % 2][:].bitcast(F32), ALU.subtract).then_inc(w_lo_done, 1)

            def keep_mods(n0, n):
                dve.wait_ge(mod_used, n0 + n)
                c = n0 % NMOD
                V.tensor_tensor(modv[:, n0:n0 + n], pmod[:, 2 * c:2 * (c + n)].rearrange("p (n c) -> p n c", c=2),
                                kp("bmod", n0, n).unsqueeze(2).to_broadcast([P, n, 2]), ALU.add).then_inc(mod_kept, 1)

            def norm(n, kept_mods):
                l, second = divmod(n, 2)
                sh = NMOD * l + 24 * second
                dve.wait_ge(mod_kept, kept_mods)
                step(V.scalar_tensor_tensor(gainA[:], modv[:, sh + 8:sh + 16], 1.0,
                                            kp(("norm1", "norm2")[second], KT * l, KT).unsqueeze(2).to_broadcast([P, KT, 2]),
                                            ALU.add, ALU.mult))
                dve.wait_ge(pm_free, M_NORM[n] + 1)
                step(V.reciprocal(tB(0), tB(0)))

                def scale(kt):
                    if kt >= 2:
                        dve.wait_ge(h_ready, KT * n + kt - 1)
                    for x, (a, b) in enumerate(((0, LAT), (LAT, TOK))):
                        last = V.scalar_tensor_tensor(tA(kt % 2)[:, a:b], xT[:, kt, a:b], gainA[:, kt, x:x + 1], tB(0)[:, a:b],
                                                      ALU.mult, ALU.mult)
                    last.then_inc(scaled, 1)

                scale(0)
                for kt in range(KT):
                    if kt < KT - 1:
                        scale(kt + 1)
                    dve.wait_ge(h_hi_done, KT * n + kt + 1)
                    for x, (a, b) in enumerate(((0, LAT), (LAT, TOK))):
                        last = V.scalar_tensor_tensor(h_lo[:, kt, a:b], tA(kt % 2)[:, a:b], modv[:, sh + kt, x:x + 1],
                                                      h_hi[:, kt, a:b].bitcast(F32), ALU.add, ALU.subtract)
                    last.then_inc(h_ready, 1)

            def conv(n):
                s, t = S_IN[0] + 3 + 3 * n, T_IN[0] + 6 + 6 * n
                lo(s + 1)
                lo(s + 2)
                for c in range(2):
                    taken(dve, t + c)
                    dve.wait_ge(tile_done, t + 2 + c + 1)
                    V.tensor_tensor(two(tB(c)), banks(pp[(t + c) % 2]), two(tA(c)), ALU.mult).then_inc(tile_free[(t + c) % 2], 1)
                lo(s + 3)
                for c in range(2):
                    u, y, g = tB(c), tA(c), 2 * n + c
                    taken(dve, t + 2 + c)
                    w = [kp("conv", 4 * x + g, 1) for x in range(3)]
                    step(V.tensor_scalar(y, u, w[1], None, ALU.mult))
                    for a, b in ((0, LAT), (LAT, TOK)):
                        step(V.scalar_tensor_tensor(y[:, a + 1:b], u[:, a:b - 1], w[0], y[:, a + 1:b], ALU.mult, ALU.add))
                        step(V.scalar_tensor_tensor(y[:, a:b - 1], u[:, a + 1:b], w[2], y[:, a:b - 1], ALU.mult, ALU.add))
                    dve.wait_ge(tile_done, t + 4 + c + 1)
                    V.tensor_tensor(two(tB(c)), banks(pp[(t + c) % 2]), two(y), ALU.mult).then_inc(tile_free[(t + c) % 2], 1)
                for c in range(2):
                    g = 2 * n + c
                    dve.wait_ge(prod_hi, g + 1)
                    V.tensor_tensor(mix_lo[:, 4 + g], tB(c), mix_hi[:, 4 + g].bitcast(F32), ALU.subtract).then_inc(prod_lo, 1)

            def pool_tile(g):
                x, w = tA(g % 2, PADW), 2 << g
                if g:
                    dve.wait_ge(pm_done, M_POOL + g)
                taken(dve, T_IN[1] + 6 + g)
                src, r, lo_, hi_ = x, 0, 0, PADW
                for m in range(g + 1):
                    dst = tB(m % 2, PADW)
                    a, b = (1, 0) if m == 0 else (2 ** (m - 1), 2 ** (m - 1))
                    lo_, hi_ = lo_ + a, hi_ - b
                    step(V.tensor_tensor(dst[:, lo_:hi_], src[:, lo_ - a:hi_ - a], src[:, lo_ + b:hi_ + b], ALU.add))
                    src = dst
                for x0, n in ((8, LAT), (CTX0, CTX)):
                    for side, at in enumerate((x0, x0 + n - 8)):
                        step(V.tensor_tensor(src[:, at:at + 8], src[:, at:at + 8], kp("edge", 16 * g + 8 * side, 8), ALU.mult))
                out = tB((g + 1) % 2, PADW)
                V.scalar_tensor_tensor(out[:, 8:CTX0 + CTX], src[:, 8:CTX0 + CTX], 1.0 / w, x[:, 8:CTX0 + CTX], ALU.mult,
                                       ALU.subtract).then_inc(pooled, 1)

            def pool_lo(g):
                dve.wait_ge(pool_hi, g + 1)
                V.scalar_tensor_tensor(two(mix_lo[:, 4 + g]), banks(pm), kp("pscale", g, 1), two(mix_hi[:, 4 + g].bitcast(F32)),
                                       ALU.mult, ALU.subtract).then_inc(pm_free, 1)

            def project_in(l):
                for n in range(3):
                    lo(S_IN[l] + n + 1)
                if l == 0:
                    for n in range(2):
                        conv(n)
                    return
                step(V.memset(tmpB[:], 0.0))
                V.memset(tA(0, PADW), 0.0).then_inc(pads_zero, 1)
                V.memset(tA(1, PADW), 0.0).then_inc(pads_zero, 1)
                for n in range(2):
                    lo(S_IN[l] + 4 + n)
                for g in range(5):
                    if g < 4:
                        pool_tile(g)
                    if g:
                        pool_lo(g - 1)

            def qk_norm(l):
                dve.wait_ge(mixer_in, 16)
                for j in range(5):
                    z = q[:, j] if j < 4 else k[:]
                    r = tB(j % 2)
                    dve.wait_ge(pm_free, M_VAR[l] + j + 1)
                    step(V.reciprocal(r, r))
                    V.scalar_tensor_tensor(z, z, kp("gain", 2 * l + (j == 4), 1), r, ALU.mult, ALU.mult).then_inc(zn_ready, 1)
                    dve.wait_ge(po_done, O_ROT[l] + j + 1)
                    V.tensor_tensor(r[:, 0:LAT], po[:], mx("sin"), ALU.mult).then_inc(po_free, 1)
                    step(V.tensor_tensor(z[:, 0:LAT], z[:, 0:LAT], mx("cos"), ALU.mult))
                    dve.wait_ge(po_free, O_ROT[l] + j + 1)
                    ins = V.tensor_tensor(z[:, 0:LAT], z[:, 0:LAT], r[:, 0:LAT], ALU.add)
                    ins.then_inc(rotated, 1)
                dve.wait_ge(rotated, 5 * l + 5)
                V.tensor_scalar(nsink[:], kp("sink"), -1.0, None, ALU.mult).then_inc(qk_ready, 1)

            def attention(l):
                def maxes(c, i):
                    g, b = divmod(c, TT)
                    n = sum(x[2] for x in attn_keys(l, b))
                    dve.wait_ge(tile_done, i * 10 + (T_ATT[l] + c + 1))
                    V.tensor_reduce(soft[:, c % 2, 0:1], pp[(T_ATT[l] + c) % 2][:, 0:n], AX, ALU.max).then_inc(rowmax_done, 1)
                    dve.wait_ge(rowmax_done, i * 10 + (40 * l + c + 1))
                    if l == 0:
                        ins = V.tensor_scalar(soft[:, c % 2, 1:2], soft[:, c % 2, 0:1], -SCALE, None, ALU.mult)
                    else:
                        ins = V.scalar_tensor_tensor(soft[:, c % 2, 1:2], soft[:, c % 2, 0:1], -SCALE,
                                                     nsink[:, bass.ds(i + 4 * g, 1)], ALU.mult, ALU.min)
                    ins.then_inc(negmax_done, 1)

                def divide(c, i):
                    n = sum(x[2] for x in attn_keys(l, c % TT))
                    taken(dve, T_ATT[l] + c, i, 10)
                    if l == 1:
                        V.tensor_tensor(soft[:, c % 2, 2:3], soft[:, c % 2, 2:3], soft[:, c % 2, 4:5], ALU.add).then_inc(den_done, 1)
                        dve.wait_ge(den_done, i * 10 + (c + 1))
                    V.reciprocal(soft[:, c % 2, 3:4], soft[:, c % 2, 2:3]).then_inc(rsum_done, 1)
                    dve.wait_ge(rsum_done, i * 10 + (40 * l + c + 1))
                    V.tensor_scalar(probs[c % 2][:, 0:n], probs[c % 2][:, 0:n], soft[:, c % 2, 3:4], None, ALU.mult
                                    ).then_inc(p_ready, 1)

                def out_lo(c, i):
                    g, b = divmod(c, TT)
                    rows = slice(g * HD, g * HD + HD)
                    dve.wait_ge(o_hi_done, i * 10 + (40 * l + c + 1))
                    at = (rows, bass.ds(i, 1), slice(b * P, (b + 1) * P))
                    V.tensor_tensor(mix_lo[at], po[rows, 0:P].unsqueeze(1), mix_hi[at].bitcast(F32), ALU.subtract).then_inc(po_free, 1)

                with dve.Fori(0, 4) as i:
                    dve.wait_ge(tile_done, i * 10 + T_ATT[l])
                    V.tensor_copy(qcur[:].unsqueeze(1), q[:, bass.ds(i, 1)]).then_inc(q_ready, 1)
                    if l == 1:
                        for g in range(2):
                            V.tensor_copy(sinkcur[:, g:g + 1], kp("sink")[:, bass.ds(i + 4 * g, 1)])
                    maxes(0, i)
                    for c in range(10):
                        if c < 9:
                            maxes(c + 1, i)
                        divide(c, i)
                        if c:
                            out_lo(c - 1, i)
                    out_lo(9, i)

            def add_tile(t, d, gate, it=0, tstep=0, dyn=None):
                dve.wait_ge(tile_done, it * tstep + (t + 1))
                for a, b, x in pieces:
                    last = V.scalar_tensor_tensor(xT[:, d, a:b], pp[t % 2][:, at_bank(a, b)], modv[:, gate + d, x:x + 1], xT[:, d, a:b],
                                                  ALU.mult, ALU.add)
                last.then_inc(tile_free[t % 2], 1)

            def project_out(l):
                for n in range(4):
                    s = S_OUT[l] + n
                    if s < S_LAST:
                        lo(s + 1)
                    for c in range(2):
                        add_tile(T_OUT[l] + 2 * n + c, 2 * n + c, NMOD * l + 16)

            def ffn():
                s, t, p = S_FFN, T_FFN, P_FFN
                for hidden in FFN_PARTS:
                    with dve.Fori(0, hidden // 2) as i:
                        lo(s + 1, i, 2)
                        lo(s + 2, i, 2)
                        for c in range(2):
                            taken(dve, t + c, i, 4)
                            dve.wait_ge(tile_done, i * 4 + (t + 2 + c + 1))
                            V.tensor_tensor(two(tB(c)), banks(pp[(t + c) % 2]), two(tA(c)), ALU.mult).then_inc(tile_free[(t + c) % 2], 1)
                        for c in range(2):
                            dve.wait_ge(prod_hi, i * 2 + (p + c + 1))
                            at = (slice(None), bass.ds(i * 2 + c, 1))
                            V.tensor_tensor(fh_lo[at], tB(c).unsqueeze(1), fh_hi[at].bitcast(F32), ALU.subtract).then_inc(prod_lo, 1)
                    s, t, p = s + hidden, t + 2 * hidden, p + hidden
                    for n in range(4):
                        lo(s + 1)
                        for c in range(2):
                            add_tile(t + c, 2 * n + c, 40)
                        s, t = s + 1, t + 2

            def routing():
                dve.wait_ge(rw_hi_done, 1)
                V.tensor_tensor(rw_lo[:], ro("router"), rw_hi[:].bitcast(F32), ALU.subtract).then_inc(rw_ready, 1)

                def row(i):
                    return rt[:, i].rearrange("p (t e) -> p t e", e=NE)

                def col(i):
                    return rc[:, i, 0:TT]

                def wide(a):
                    return a.unsqueeze(2).to_broadcast([P, TT, NE])

                def every(a, n=TT):
                    return a.unsqueeze(1).to_broadcast([P, n, a.shape[-1]])

                dve.wait_ge(pm_done, M_LOGIT + 1)
                ins = V.tensor_tensor(row(0), pm[:, 0:TT * NE].rearrange("p (t e) -> p t e", e=NE), every(kp("rbias")), ALU.add)
                ins.then_inc(pm_free, 1)
                dve.wait_ge(pm_free, M_LOGIT + 1)
                for n in range(1, 2 * TT, 2):
                    dve.wait_ge(tile_done, T_TOK + n + 1)
                    V.tensor_copy((tok_hi if n < TT else tok_lo)[:, n % TT], pp[n % 2][:, :]).then_inc(tile_free[n % 2], 1)
                for x in range(2):
                    step(V.tensor_reduce(col(x), row(0), AX, ALU.max))
                    step(V.tensor_tensor(row(1), row(0), wide(col(x)), ALU.is_equal))
                    step(V.tensor_tensor(row(1), row(1), every(ro("desc")), ALU.mult))
                    step(V.tensor_reduce(col(2), row(1), AX, ALU.max))
                    step(V.tensor_tensor(row(2 + x), row(1), wide(col(2)), ALU.is_equal))
                    if x == 0:
                        step(V.scalar_tensor_tensor(row(0), row(2), NEG, row(0), ALU.mult, ALU.add))
                V.tensor_tensor(col(4), col(1), col(0), ALU.subtract).then_inc(gap_ready, 1)
                V.tensor_tensor(row(11), row(2), row(3), ALU.add).then_inc(mask_ready, 1)
                dve.wait_ge(mask_ready, 1)
                dve.wait_ge(gap_exp, 1)
                step(V.tensor_scalar(col(3), col(5), 1.0, None, ALU.add))
                step(V.reciprocal(col(0), col(3)))
                step(V.tensor_tensor(col(1), col(5), col(0), ALU.mult))
                step(V.tensor_tensor(row(4), row(2), wide(col(0)), ALU.mult))
                step(V.tensor_tensor(row(5), row(3), wide(col(1)), ALU.mult))
                step(V.tensor_tensor(row(4), row(4), row(5), ALU.add))
                dve.wait_ge(pm_done, M_RANK + 1)
                step(V.tensor_copy(rt[:, 6], pm[:, 0:TT * NE]))
                ins = V.tensor_copy(rt[:, 7, 0:NE], pm[:, TT * NE:(TT + 1) * NE])
                ins.then_inc(pm_free, 1)
                dve.wait_ge(pm_free, M_RANK + 1)
                step(V.scalar_tensor_tensor(row(8), row(6), 1.0, row(11), ALU.add, ALU.mult))
                for r in range(ROUNDS):
                    step(V.tensor_scalar(rcand[:, :, r * NE:(r + 1) * NE], row(8), -1.0 - CAP * r, None, ALU.add))
                flag, rank = rc[:, 0], rc[:, 1]
                step(V.tensor_tensor(flag.rearrange("p (r e) -> p r e", e=NE), every(rt[:, 7, 0:NE], ROUNDS),
                                     ro("thr").rearrange("p (r e) -> p r e", e=NE), ALU.is_gt))
                big = rbig[:, 0:NCAND * NCAND].rearrange("p (a b) -> p a b", b=NCAND)
                step(V.tensor_tensor(big, ro("u24").rearrange("p (a b) -> p a b", b=NCAND), every(flag, NCAND), ALU.mult))
                step(V.tensor_reduce(rank, big, AX, ALU.add))
                step(V.tensor_tensor(rsel[:], every(rank, MAX_ITEMS), ro("jidx").rearrange("p (j i) -> p j i", i=NCAND), ALU.is_equal))
                step(V.tensor_tensor(rsel[:], rsel[:], every(flag, MAX_ITEMS), ALU.mult))
                small = rbig[:, 0:MAX_ITEMS * NCAND].rearrange("p (j i) -> p j i", i=NCAND)
                step(V.tensor_tensor(small, rsel[:], every(ro("cand"), MAX_ITEMS), ALU.mult))
                step(V.tensor_reduce(rc[:, 2, 0:MAX_ITEMS], small, AX, ALU.add))
                step(V.tensor_reduce(rc[:, 2, MAX_ITEMS:MAX_ITEMS + 1], flag, AX, ALU.add))
                step(V.tensor_copy(item_no[:], rc[:, 2, 0:MAX_ITEMS + 1]))
                big = rbig[:].rearrange("p (t j i) -> p t j i", t=TT, j=MAX_ITEMS)

                def per_item(out):
                    for t in range(TT):
                        last = V.tensor_tensor(big[:, t], rsel[:], every(rcand[:, t], MAX_ITEMS), ALU.mult)
                    step(last)
                    return V.tensor_reduce(out[:], big, AX, ALU.add)

                step(per_item(item_pos))
                for r in range(ROUNDS):
                    last = V.tensor_copy(rcand[:, :, r * NE:(r + 1) * NE], row(4))
                step(last)
                per_item(item_gate).then_inc(routed, 1)
                dve.wait_ge(iota_in, 16)

            def experts():
                n_items = items(dve)
                with dve.Fori(0, n_items) as j:
                    dve.wait_ge(tile_done, j * ITEM_TILES + T_MOE)
                    for t in range(TT):
                        last = V.tensor_scalar(onehot[:, t], iota[:], item_pos[:, t, bass.ds(j, 1)], None, ALU.is_equal)
                    last.then_inc(onehot_ready, 1)
                    lo(S_MOE, j, ITEM_SLABS)
                    for kt in range(KT):
                        dve.wait_ge(tile_done, j * ITEM_TILES + (T_MOE + kt + 1))
                        V.tensor_copy(g_hl[:, kt].rearrange("p x c -> p (x c)"), pp[kt % 2][:, 0:2 * CAP]
                                      ).then_inc(tile_free[kt % 2], 1)
                    t = T_MOE + KT
                    with dve.Fori(0, 4) as i:
                        for c in (1, 0):
                            dve.wait_ge(w_hi_done, j * ITEM_SLABS + i * 2 + (S_MOE + 3 - c))
                            V.tensor_tensor(w_lo[c][:], raw[c][:], w_hi[c][:].bitcast(F32), ALU.subtract).then_inc(w_lo_done, 1)
                        for c in range(2):
                            dve.wait_ge(tile_free[c], j * (ITEM_TILES // 2) + i * 2 + (t // 2 + 1))
                            dve.wait_ge(tile_done, j * ITEM_TILES + i * 4 + (t + 2 + c + 1))
                            V.tensor_tensor(tB(c, CAP), pp[(t + c) % 2][:, 0:CAP], tA(c, CAP), ALU.mult
                                            ).then_inc(tile_free[(t + c) % 2], 1)
                        for c in range(2):
                            dve.wait_ge(prod_hi, j * 8 + i * 2 + (P_MOE + c + 1))
                            at = (slice(None), bass.ds(i * 2 + c, 1))
                            V.tensor_tensor(e_lo[at], tB(c, CAP).unsqueeze(1), e_hi[at].bitcast(F32), ALU.subtract).then_inc(prod_lo, 1)
                    t += 16
                    for n in range(4):
                        if n < 3:
                            lo(S_MOE + 9 + n, j, ITEM_SLABS)
                        for sl in range(2):
                            dve.wait_ge(yhi_done, j * 8 + (2 * n + sl + 1))
                            at = (slice(None), sl, slice(n * SLAB, (n + 1) * SLAB))
                            ins = V.scalar_tensor_tensor(y_lo[at], pp[sl][:, 0:SLAB], gslot[:, sl:sl + 1], y_hi[at].bitcast(F32),
                                                         ALU.mult, ALU.subtract)
                            ins.then_inc(tile_free[sl], 1)
                    t += 8
                    for d in range(KT):
                        add_tile(t + d, d, NMOD + 40, j, ITEM_TILES)

            V.memset(eps[:], EPS).then_inc(eps_set, 1)
            dve.wait_ge(kept_in, 16)
            lo(0)
            keep_mods(0, 16)
            norm(0, 1)
            keep_mods(16, 16)
            project_in(0)
            qk_norm(0)
            keep_mods(32, 16)
            attention(0)
            project_out(0)
            norm(1, 3)
            keep_mods(48, 16)
            ffn()
            norm(2, 4)
            keep_mods(64, 16)
            project_in(1)
            qk_norm(1)
            keep_mods(80, 16)
            attention(1)
            project_out(1)
            norm(3, 6)
            routing()
            experts()


def shape_constants():
    import numpy as np

    f = np.float32
    eye = np.eye(P, dtype=f)
    rot = np.zeros((P, P), f)
    for n in range(P):
        quarter = HD // 4
        if n % (2 * quarter) < quarter:
            rot[n + quarter, n] = -1
        else:
            rot[n - quarter, n] = 1
    blk = np.kron(np.eye(P // HD), np.ones((HD, HD))).astype(f)
    a, b = np.arange(P)[:, None], np.arange(P)[None, :]
    rows = np.repeat(np.arange(LAT // 64, dtype=f), 64)
    cols = np.tile(np.arange(64, dtype=f), LAT // 64)
    inv = f(10000.0) ** (-np.arange(HD // 4, dtype=f) / f(HD // 4))
    ang = np.stack([rows[:, None] * inv, cols[:, None] * inv], axis=1)
    per = np.concatenate([ang[:, 0], ang[:, 0], ang[:, 1], ang[:, 1]], axis=1).T
    per = np.concatenate([per, per], axis=0)
    edge = np.ones((4, 2, 8), f)
    for g in range(4):
        w = 2 << g
        for x in range(8):
            edge[g, 0, x] = f(w) / f(min(w, x + w // 2))
            edge[g, 1, x] = f(w) / f(min(w, w // 2 + 8 - x))
    cand = np.arange(NCAND)
    thr = np.where(cand < NE, -1, CAP * (cand // NE))
    wide = {
        "ident": eye, "ones": np.ones((P, P)), "rot": rot, "blk": blk, "upper": (a < b),
        "mprev": np.where(b >= a, 0, NEG), "mnext": np.where(b <= a, 0, NEG),
        "cos": np.cos(per), "sin": np.sin(per), "edge": edge.reshape(-1), "iota": np.arange(CAP),
        "desc": NE - np.arange(NE), "thr": thr, "cand": cand % NE,
        "u24": (cand[None, :] < cand[:, None]).reshape(-1), "jidx": np.repeat(np.arange(MAX_ITEMS), NCAND),
    }
    return {n: np.broadcast_to(np.asarray(v, f), (P, np.asarray(v).shape[-1])) for n, v in wide.items()}


def lay_out(x):
    import numpy as np

    f = np.float32
    consts = shape_constants()

    def columns(a):
        return np.ascontiguousarray(a.reshape(-1, P).T)

    def slabs(w, order=None):
        kk, n = w.shape
        w = w.reshape(kk // P, P, n // SLAB, SLAB).transpose(2, 1, 0, 3)
        out = np.zeros((n // SLAB, P, 8, SLAB), f)
        out[:, :, :kk // P] = w
        return out.reshape(n // SLAB, P, 8 * SLAB)

    heads = np.arange(512).reshape(2, 4, HD).transpose(1, 0, 2).reshape(-1)
    ev, od = x["ev_w_in"][0], x["od_w_in"][0]
    bg, cg, xa = ev[:, 0:512], ev[:, 512:1024], ev[:, 1024:1536]
    parts = [slabs(ev[:, 1536 + heads]), slabs(ev[:, 2048:2304])]
    for n in range(2):
        parts += [slabs(w[:, n * SLAB:(n + 1) * SLAB]) for w in (xa, cg, bg)]
    eo, oo = x["ev_w_out"][0], x["od_w_out"][0]
    parts.append(slabs(np.concatenate([eo[512 + heads], eo[0:512]])))
    w1, w3, w2 = x["ffn_w1"][0], x["ffn_w3"][0], x["ffn_w2"][0]
    at = 0
    for hidden in FFN_PARTS:
        for n in range(hidden // 2):
            c = slice(at + n * SLAB, at + (n + 1) * SLAB)
            parts += [slabs(w1[:, c]), slabs(w3[:, c])]
        parts.append(slabs(w2[at:at + hidden * P]))
        at += hidden * P
    parts += [slabs(od[:, heads]), slabs(od[:, 512:1280])]
    parts.append(slabs(np.concatenate([oo[heads], oo[512:]])))
    for e in range(NE):
        a, b = slabs(x["moe_w1"][0, e]), slabs(x["moe_w3"][0, e])
        parts += [np.stack([a, b], axis=1).reshape(8, P, -1), slabs(x["moe_w2"][0, e])]
    ws = np.concatenate(parts)
    wmod = x["w_mod"].reshape(2, KT, P, NMOD, P).transpose(0, 3, 2, 1, 4).reshape(2 * NMOD, P, KT * P)
    tokens = np.concatenate([x["x_sample"][0], x["x_prompt"][0]])
    xT = tokens.T.reshape(KT, P, TOK).transpose(1, 0, 2)

    def gain(a):
        return np.concatenate([a[0], a[0]])[:, None]

    def rows(a):
        return np.broadcast_to(a.reshape(1, -1), (P, a.size))

    kc = x["cache_k"][0].transpose(0, 1, 3, 2).reshape(2, P, PAST).transpose(1, 0, 2).reshape(P, -1)
    vc = x["cache_v"][0].transpose(0, 2, 1, 3).reshape(2, 2, P, P).transpose(2, 0, 1, 3).reshape(P, -1)
    data = {
        "bmod": columns(x["b_mod"]), "norm1": columns(x["norm1"]), "norm2": columns(x["norm2"]),
        "cond": np.stack([columns(x["c"]), columns(x["c_ctx"])], axis=2).reshape(P, -1),
        "conv": columns(x["ev_conv"][0]), "pscale": columns(x["od_pool_scale"]),
        "gain": np.concatenate([gain(x[n]) for n in ("ev_q_norm", "ev_k_norm", "od_q_norm", "od_k_norm")], axis=1),
        "sink": rows(x["od_sink"]), "rbias": rows(x["moe_router_b"]), "kc": kc, "vc": vc,
        "poolw": x["od_pool_w"][0].transpose(1, 0, 2).reshape(P, -1),
        "router": x["moe_router"][0].reshape(KT, P, NE).transpose(1, 0, 2).reshape(P, -1),
    }
    data.update(consts)

    def pack(table):
        return np.concatenate([data[n] for n, _ in table], axis=1)

    return {"xT": xT, "kept": pack(_KEPT), "mixer": pack(_MIXER), "route": pack(_ROUTE), "iota": data["iota"],
            "wmod": wmod, "ws": ws}


def kernel(**inputs):
    import numpy as np
    import concourse.bacc as bacc
    from concourse.bass_utils import run_bass_kernel_spmd

    given = {n: np.asarray(a) for n, a in inputs.items()}
    nc = bacc.Bacc("TRN2", target_bir_lowering=False, num_devices=1)
    arrays, args = {}, []
    for name, a in lay_out(given).items():
        a = np.ascontiguousarray(a)
        arrays[f"in_{name}"] = a
        args.append(nc.dram_tensor(f"in_{name}", a.shape, mybir.dt.from_np(a.dtype), kind="ExternalInput").ap())
    for name, shape in (("out_y", (P, KT, TOK)), ("out_k", (2, P, CTX)), ("out_v", (2, P, CTX))):
        args.append(nc.dram_tensor(name, shape, F32, kind="ExternalOutput").ap())
    build(nc, *args)
    got = run_bass_kernel_spmd(nc, [arrays], core_ids=[0]).results[0]
    y = got["out_y"].transpose(2, 1, 0).reshape(TOK, D)
    new_k, new_v = (got[n].reshape(1, 2, 2, HD, CTX).transpose(0, 1, 2, 4, 3) for n in ("out_k", "out_v"))
    return (np.ascontiguousarray(y[None, LAT:]), np.ascontiguousarray(y[None, :LAT]),
            np.ascontiguousarray(new_k), np.ascontiguousarray(new_v))
```

```python
from contextlib import ExitStack

import concourse.bass as bass
from concourse import mybir

F32 = mybir.dt.float32
F32R = mybir.dt.float32r
I32 = mybir.dt.int32
ALU = mybir.AluOpType
ACT = mybir.ActivationFunctionType
AX = mybir.AxisListType.X

P = 128
D = 1024
KT = D // P
LAT, CTX = 512, 128
TOK = LAT + CTX
TT = TOK // P
HALF = TOK // 2
PAST = 256
HD = 64
SCALE = HD ** -0.5
EPS = 1e-6
NMOD = 6 * D // P
SLAB = 256
NE = 8
MOD_FIRST = 16
CAP = 256
ROUNDS = -(-TOK // CAP)
NCAND = ROUNDS * NE
MAX_ITEMS = NE + 2 * TOK // (CAP + 1)
ROOM = MAX_ITEMS + 1
FFN_PARTS = (8, 8, 6)
PADW = 8 + LAT + 16 + CTX + 8
CTX0 = 8 + LAT + 16
NEG = -1e30
KEYS = PAST + TOK
KEY_TILES = KEYS // P
UNITS = 10
CTX_UNITS = 8
STEPS = 8 * 6 + 2

S_IN = (0, 47)
S_OUT = (9, 52)
S_FFN = 13
S_MOE = 56
T_IN = (0, 134)
T_ATT = (18, 144)
T_OUT = (58, 184)
T_FFN = 66
T_TOK = 192
T_MOE = 202
ITEM_TILES = KT + 16 + 8 + KT
ITEM_SLABS = 12
T_ITEM = T_MOE + KT
GATHER_AT = (16, 17, 20, 21, 26, 27, 30, 31)
OUT_AT = (18, 22, 24, 28)
COMBINE_AT = 32
M_NORM = (0, 7, 8, 19)
M_V = (1, 13)
M_POOL = 9
M_VAR = (2, 14)
M_LOGIT, M_RANK, M_MOE = 20, 21, 22
O_ROT = (0, 15)
O_ATT = (5, 20)
P_CONV, P_FFN, P_MOE = 0, 4, 26

_KEPT = [("bmod", 2 * NMOD), ("norm1", 2 * KT), ("norm2", 2 * KT), ("conv", 12),
         ("pscale", 4), ("gain", 4), ("sink", 8), ("rbias", NE), ("edge", 64), ("ident", P), ("ones", P)]
_MIXER = [("kc", 2 * PAST), ("vc", 2 * PAST), ("poolw", 4 * P), ("rot", P), ("blk", P), ("mprev", P),
          ("mnext", P), ("cos", LAT), ("sin", LAT)]
_ROUTE = [("router", KT * NE), ("upper", P), ("desc", NE), ("thr", NCAND), ("cand", NCAND),
          ("u24", NCAND * NCAND), ("jidx", ROOM * NCAND)]


def offsets(table):
    out, at = {}, 0
    for name, n in table:
        out[name] = (at, n)
        at += n
    return out, at


KEPT, NKEPT = offsets(_KEPT)
MIXER, NMIXER = offsets(_MIXER)
ROUTE, NROUTE = offsets(_ROUTE)


def attn_blocks(layer, u):
    if u >= CTX_UNITS:
        return [[(PAST + LAT, CTX, None)]] * 4
    if layer == 0:
        return [[(0, 512, None), (512, 256, None)]] * 4
    out = []
    for b in range(4):
        out.append([(0, PAST, None)])
        for o, mask in ((-1, 0), (0, None), (1, 1)):
            if 0 <= b + o < 4:
                out[b].append((PAST + (b + o) * P, P, mask))
    return out


def attn_tiles(layer, u):
    if u >= CTX_UNITS:
        return [((PAST + LAT) // P, 0, 4, {})]
    out = []
    for t in range((PAST + LAT) // P):
        b = t - PAST // P
        if layer == 0 or b < 0:
            out.append((t, 0, 4, {}))
        else:
            masks = {b + o: m for o, m in ((-1, 0), (1, 1)) if 0 <= b + o < 4}
            out.append((t, max(b - 1, 0), min(b + 2, 4), masks))
    return out


def build(nc, xT_d, kept_d, mixer_d, route_d, iota_d, cond_d, wmod_d, ws_d, y_d, newk_d, newv_d):
    with ExitStack() as ctx:
        def sb(name, shape, dt=F32, scope=ctx):
            return scope.enter_context(nc.sbuf_tensor(name, shape, dt))

        def sem(name):
            return ctx.enter_context(nc.semaphore(name))

        xT = sb("xT", [P, KT, TOK])
        raw = [sb(f"raw{i}", [P, 8, SLAB]) for i in range(2)]
        w_hi = [sb(f"w_hi{i}", [P, 8, SLAB], F32R) for i in range(2)]
        w_lo = [sb(f"w_lo{i}", [P, 8, SLAB], F32R) for i in range(2)]
        modraw = [sb(f"modraw{i}", [P, D]) for i in range(2)]
        kept = sb("kept", [P, NKEPT])
        modv = sb("modv", [P, 2 * NMOD, 2])
        gainA = sb("gainA", [P, KT, 2])
        scond = sb("scond", [P, 2, D])
        tmpA = sb("tmpA", [P, 2 * PADW])
        tmpB = sb("tmpB", [P, 2 * PADW])

        def kp(name, a=0, n=None):
            at, full = KEPT[name]
            return kept[:, at + a:at + (full if n is None else a + n)]

        def tA(c, n=TOK):
            return tmpA[:, c * PADW:c * PADW + n]

        def tB(c, n=TOK):
            return tmpB[:, c * PADW:c * PADW + n]

        with ExitStack() as r:
            mod_first = [sb("mod_first0", [P, 8, D], F32, r)]
            with ExitStack() as r2:
                mod_first.append(sb("mod_first1", [P, 8, D], F32, r2))
        with ExitStack() as r:
            h_hi = sb("h_hi", [P, KT, TOK], F32R, r)
            h_lo = sb("h_lo", [P, KT, TOK], F32R, r)
            with ExitStack() as r2:
                mix_hi = sb("mix_hi", [P, KT, TOK], F32R, r2)
                mix_lo = sb("mix_lo", [P, KT, TOK], F32R, r2)
                q = sb("q", [P, 4, TOK], F32, r2)
                k = sb("k", [P, TOK], F32, r2)
                v = sb("v", [P, TOK], F32, r2)
            with ExitStack() as r2:
                fh_hi = sb("fh_hi", [P, 8, TOK], F32R, r2)
                fh_lo = sb("fh_lo", [P, 8, TOK], F32R, r2)
            with ExitStack() as r2:
                tok_hi = sb("tok_hi", [P, TT, D], F32R, r2)
                tok_lo = sb("tok_lo", [P, TT, D], F32R, r2)
                with ExitStack() as r3:
                    y_hi = sb("y_hi", [P, 2, D], F32R, r3)
                    y_lo = sb("y_lo", [P, 2, D], F32R, r3)
                route = sb("route", [P, NROUTE], F32, r2)
                rw_hi = sb("rw_hi", [P, KT * NE], F32R, r2)
                rw_lo = sb("rw_lo", [P, KT * NE], F32R, r2)
                rt = sb("rt", [P, 12, TT * NE], F32, r2)
                rc = sb("rc", [P, 6, NCAND], F32, r2)
                rsel = sb("rsel", [P, ROOM, NCAND], F32, r2)
                rbig = sb("rbig", [P, TT * ROOM * NCAND], F32, r2)
                rcand = sb("rcand", [P, TT, NCAND], F32, r2)
        with ExitStack() as r:
            keysA = [sb(f"keysA{i}", [P, KEYS], F32R, r) for i in range(2)]
            keysB = [sb(f"keysB{i}", [P, KEYS], F32R, r) for i in range(2)]
            vals = [sb(f"vals{i}", [P, KEY_TILES, P], F32, r) for i in range(2)]
            qA = [sb(f"qA{i}", [P, 512], F32R, r) for i in range(2)]
            qB = [sb(f"qB{i}", [P, 512], F32R, r) for i in range(2)]
            probs = [sb(f"probs{i}", [P, 512], F32, r) for i in range(3)]
            masks_r = sb("masks_r", [P, 2, P], F32R, r)
            ident_r = sb("ident_r", [P, P], F32R, r)
            den_row = sb("den_row", [P, 2, P], F32, r)
        with ExitStack() as r:
            g_hl = sb("g_hl", [P, KT, 2, CAP], F32R, r)
            e_hi = sb("e_hi", [P, 8, CAP], F32R, r)
            e_lo = sb("e_lo", [P, 8, CAP], F32R, r)
        sb("region1", [P, 2 * KT * TOK])
        sb("region2", [P, 2 * KT * TOK + 4 * TOK + 3 * TOK])

        with ExitStack() as r:
            mixer = sb("mixer", [P, NMIXER], F32, r)
        iota = sb("iota", [P, CAP])
        onehot = sb("onehot", [P, TT, CAP], F32R)
        selT = sb("selT", [P, 2, TOK], F32R)
        sb("region3_rest", [P, NMIXER - CAP - TT * CAP - 2 * TOK])

        def mx(name, a=0, n=None):
            at, full = MIXER[name]
            return mixer[:, at + a:at + (full if n is None else a + n)]

        def ro(name, a=0, n=None):
            at, full = ROUTE[name]
            return route[:, at + a:at + (full if n is None else a + n)]

        ident, ones = kp("ident"), kp("ones")
        rowmax = sb("rowmax", [P, 2, 4])
        rowmax_r = sb("rowmax_r", [P, 2, 4], F32R)
        item_pos = sb("item_pos", [P, TT, ROOM])
        item_gate = sb("item_gate", [P, TT, ROOM])
        item_no = sb("item_no", [P, ROOM + 1], I32)
        gslot = sb("gslot", [P, 2])
        sink8 = sb("sink8", [P, 8])
        sinkcur = sb("sinkcur", [P, 2, 4])
        eps = sb("eps", [P, 1])

        pp = [ctx.enter_context(nc.psum_tensor(f"pp{i}", [P, 1024], F32)) for i in range(2)]
        pm = ctx.enter_context(nc.psum_tensor("pm", [P, 1024], F32))
        popr = ctx.enter_context(nc.psum_tensor("popr", [P, 1024], F32))
        po, prow = popr[:, 0:512], popr[:, 512:1024]
        mod_prod = popr

        kept_in, x_in, mixer_in, route_in, iota_in = (sem(n) for n in ("kept_in", "x_in", "mixer_in", "route_in", "iota_in"))
        slab_in = [sem(f"slab_in{i}") for i in range(2)]
        mod_in = [sem(f"mod_in{i}") for i in range(2)]
        w_hi_done, w_lo_done = sem("w_hi_done"), sem("w_lo_done")
        mod_first_in = [sem(f"mod_first_in{i}") for i in range(4)]
        cond_in, cond_ready, mod_used, mod_kept = (sem(n) for n in ("cond_in", "cond_ready", "mod_used", "mod_kept"))
        tile_done = sem("tile_done")
        tile_free = [sem(f"tile_free{i}") for i in range(2)]
        pm_done, pm_free, po_done, po_free = sem("pm_done"), sem("pm_free"), sem("po_done"), sem("po_free")
        sq_ready, sq_used, scaled, h_hi_done, h_ready = (sem(n) for n in ("sq_ready", "sq_used", "scaled", "h_hi_done", "h_ready"))
        prod_hi, prod_lo = sem("prod_hi"), sem("prod_lo")
        zsq_ready, zn_ready, rotated, k_hi_done = sem("zsq_ready"), sem("zn_ready"), sem("rotated"), sem("k_hi_done")
        pooled, pool_hi, pads_zero = sem("pooled"), sem("pool_hi"), sem("pads_zero")
        pool_step, cached_ready, keys_ready, q_hi_done, q_lo_done, max_ready, max_turned, max_in, sink_in = (sem(n) for n in (
            "pool_step", "cached_ready", "keys_ready", "q_hi_done", "q_lo_done", "max_ready", "max_turned", "max_in", "sink_in"))
        scores_done, exp_done, values_done, inverse_done, out_hi_done, out_kept = (sem(n) for n in (
            "scores_done", "exp_done", "values_done", "inverse_done", "out_hi_done", "out_kept"))
        kv_out, y_out = sem("kv_out"), sem("y_out")
        rw_hi_done, rw_ready, gap_ready, gap_exp, mask_ready, routed = (
            sem(n) for n in ("rw_hi_done", "rw_ready", "gap_ready", "gap_exp", "mask_ready", "routed"))
        eps_set = sem("eps_set")
        onehot_ready, slots_turned, slots_kept, yhi_done, dve_step = (
            sem(n) for n in ("onehot_ready", "slots_turned", "slots_kept", "yhi_done", "dve_step"))

        block = ctx.enter_context(nc.Block())

        def two(a):
            return a.rearrange("p (h n) -> p h n", h=2)

        def banks(pair):
            return pair[:].rearrange("p (h n) -> p h n", h=2)[:, :, 0:HALF]

        pieces = ((0, HALF, 0), (HALF, LAT, 0), (LAT, TOK, 1))

        def at_bank(a, b):
            return slice(a, b) if b <= HALF else slice(512 + a - HALF, 512 + b - HALF)

        def tiles_after(s):
            for s0, t0 in ((S_OUT[1], T_OUT[1]), (S_IN[1], T_IN[1]), (S_FFN, T_FFN), (S_OUT[0], T_OUT[0]), (0, 0)):
                if s >= s0:
                    return t0 + 2 * (s - s0) + 2

        def half(n, it=0, step=0):
            return n // 2 + it * (step // 2)

        def taken(eng, t, it=0, step=0):
            eng.wait_ge(tile_free[t % 2], half(t, it, step) + 1)

        def items(eng):
            eng.wait_ge(routed, 1)
            return eng.value_load(item_no[0:1, ROOM:ROOM + 1], min_val=NE, max_val=MAX_ITEMS)

        def norm_row(j):
            return q[:, j - 1] if j else k[:]

        def unit_rows(u):
            g = u % 2
            return slice(g * HD, g * HD + HD), slice((1 - g) * HD, (1 - g) * HD + HD)

        def unit_q(u, i):
            rows, _ = unit_rows(u)
            if u >= CTX_UNITS:
                return q[rows, :, LAT:TOK]
            return q[rows, bass.ds(i + u // 2, 1), 0:LAT].rearrange("p a (b n) -> p (a b) n", b=4)

        def unit_mix(buf, u, i):
            rows, _ = unit_rows(u)
            if u >= CTX_UNITS:
                return buf[rows, 0:4, LAT:TOK]
            return buf[rows, bass.ds(i + u // 2, 1), 0:LAT].rearrange("p a (b n) -> p (a b) n", b=4)

        def blocks(a):
            return a.rearrange("p (b n) -> p b n", b=4)

        def att_out(u):
            rows, _ = unit_rows(u)
            return tB(0, 512)[rows]

        def units(eng, unit):
            with eng.Fori(0, 3) as i:
                unit(0, 1, i)
                unit(1, 2, i)
            for u in range(6, UNITS):
                unit(u, u + 1 if u + 1 < UNITS else None, 0)

        def head(u, i):
            g = u % 2
            return slice(4 * g, 4 * g + 4) if u >= CTX_UNITS else bass.ds(i + (4 * g + u // 2), 1)

        def key_step(l, u, k=0):
            return STEPS * l + (6 * u + k if u <= CTX_UNITS else 6 * CTX_UNITS + u - CTX_UNITS + k)

        @block.sync
        def _(sp):
            sp.dma_start(kept[:], kept_d).then_inc(kept_in, 16)
            sp.dma_start(scond[:], cond_d).then_inc(cond_in, 16)
            for b in range(4):
                sp.dma_start(mod_first[b // 2][:, 4 * (b % 2):4 * (b % 2) + 4], wmod_d[4 * b:4 * b + 4].rearrange("t p k -> p t k")
                             ).then_inc(mod_first_in[b], 16)
                if b == 0:
                    sp.dma_start(xT[:], xT_d).then_inc(x_in, 16)
            for c in range(2):
                sp.dma_start(raw[c][:], ws_d[c].rearrange("p (k n) -> p k n", k=8)).then_inc(slab_in[c], 16)
            sp.dma_start(mixer[:], mixer_d).then_inc(mixer_in, 16)
            with sp.Fori(1, (S_MOE + ITEM_SLABS * NE) // 2) as i:
                for c in range(2):
                    sp.wait_ge(w_lo_done, i * 2 + (c - 1))
                    sp.dma_start(raw[c][:], ws_d[bass.ds(i * 2 + c, 1)].rearrange("a p (k n) -> (a p) k n", k=8)
                                 ).then_inc(slab_in[c], 16)
            n_items = items(sp)
            with sp.If(n_items > NE):
                with sp.Fori(NE, n_items) as j:
                    e = sp.value_load(item_no[0:1, bass.ds(j, 1)], min_val=0, max_val=NE - 1)
                    for c2 in range(ITEM_SLABS // 2):
                        for c in range(2):
                            sp.wait_ge(w_lo_done, j * ITEM_SLABS + (S_MOE + 2 * c2 + c - 1))
                            sp.dma_start(raw[c][:], ws_d[bass.ds(e * ITEM_SLABS + (S_MOE + 2 * c2 + c), 1)].rearrange(
                                "a p (k n) -> (a p) k n", k=8)).then_inc(slab_in[c], 16)
            for c in range(2):
                sp.wait_ge(w_lo_done, n_items * ITEM_SLABS + (S_MOE - 1 + c))
                sp.dma_start(raw[c][:], ws_d[S_MOE + c].rearrange("p (k n) -> p k n", k=8)).then_inc(slab_in[c], 16)
            for c in range(2):
                sp.wait_ge(tile_free[c], n_items * (ITEM_TILES // 2) + T_ITEM // 2)
            sp.dma_start(y_d, xT[:]).then_inc(y_out, 16)
            sp.wait_ge(y_out, 16)
            sp.wait_ge(kv_out, 64)

        @block.gpsimd
        def _(pool):
            for c in range(2):
                pool.dma_start(modraw[c][:], wmod_d[MOD_FIRST + c]).then_inc(mod_in[c], 16)
            steps = [0]

            def alone(ins):
                steps[0] += 1
                ins.then_inc(pool_step, 1)
                pool.wait_ge(pool_step, steps[0])

            def load_mods(a, b):
                with pool.Fori(a, b) as i:
                    for c in range(2):
                        pool.wait_ge(mod_used, i * 4 + 2 * (MOD_FIRST + c - 1))
                        pool.dma_start(modraw[c][:], wmod_d[bass.ds(i * 2 + (MOD_FIRST + c), 1)].rearrange("a p k -> (a p) k")
                                       ).then_inc(mod_in[c], 16)

            def attention(l):
                G = nc.gpsimd
                pool.wait_ge(tile_done, T_ATT[l])
                pool.wait_ge(mixer_in, 16)
                for g in range(2):
                    rows, others = unit_rows(g)
                    kc = mx("kc", l * PAST, PAST)[rows]
                    alone(G.tensor_copy(keysA[g][rows, 0:PAST], kc))
                    alone(G.tensor_copy(keysB[g][0:HD, 0:PAST], kc))
                    alone(G.tensor_tensor(keysA[g][others, 0:PAST], kc, keysA[g][rows, 0:PAST].bitcast(F32), ALU.subtract))
                    alone(G.memset(keysB[g][HD:HD + 1].bitcast(F32), -1.0))
                    alone(G.memset(vals[g][:, :, others], 1.0))
                    alone(G.tensor_copy(vals[g][:, 0:PAST // P, rows],
                                        mx("vc", l * PAST, PAST).rearrange("p (t n) -> p t n", n=P)[:, :, rows]))
                    alone(G.memset(den_row[HD:HD + 1, g, others], 1.0))
                    G.memset(den_row[HD:HD + 1, g, rows], 0.0).then_inc(out_kept, 1)
                    pool.wait_ge(out_kept, (UNITS + 2) * l + g + 1)
                alone(G.tensor_copy(masks_r[:, 0], mx("mprev")))
                alone(G.tensor_copy(masks_r[:, 1], mx("mnext")))
                G.tensor_copy(ident_r[:], ident).then_inc(cached_ready, 1)
                pool.wait_ge(cached_ready, l + 1)

                def unit(u, nu, i):
                    n = UNITS * l + u + 1
                    pool.wait_ge(po_free, i * 2 + (O_ATT[l] + u + 1))
                    pool.wait_ge(out_kept, i * 2 + ((UNITS + 2) * l + u + 2))
                    G.tensor_copy(unit_mix(mix_hi, u, i), blocks(att_out(u))).then_inc(out_hi_done, 1)
                    pool.wait_ge(out_hi_done, i * 2 + n)
                    G.tensor_tensor(unit_mix(mix_lo, u, i), blocks(att_out(u)), unit_mix(mix_hi, u, i).bitcast(F32), ALU.subtract
                                    ).then_inc(out_kept, 1)

                units(pool, unit)

            load_mods(1, 9)
            attention(0)
            load_mods(9, (2 * NMOD - MOD_FIRST) // 2)
            attention(1)
            pool.wait_ge(tile_done, T_OUT[1] + 8)
            pool.dma_start(route[:], route_d).then_inc(route_in, 16)
            pool.dma_start(iota[:], iota_d).then_inc(iota_in, 16)

        @block.tensor
        def _(pe):
            mm = nc.tensor.matmul

            def tile_slot(t, it, step):
                if t >= 2 or step:
                    pe.wait_ge(tile_free[t % 2], half(t, it, step))
                return pp[t % 2]

            def three(out, a_hi, a_lo, b_hi, b_lo, first, last, n):
                for x, y, f in ((a_hi, b_hi, first), (a_hi, b_lo, False), (a_lo, b_hi, False)):
                    end = last and x is a_lo
                    for lo, hi in ((0, HALF), (HALF, TOK)) if n == TOK else ((0, n),):
                        ins = mm(out[:, at_bank(lo, hi)], x, y[:, lo:hi], start=f, stop=end)
                return ins

            def slab(s, t, b_hi, b_lo, n=TOK, kk=KT, it=0, sstep=0, tstep=0, ready=None):
                if ready is not None:
                    outs = [tile_slot(t + c, it, tstep) for c in range(2)]
                    pe.wait_ge(w_lo_done, s + 1)
                    for kt in range(kk):
                        pe.wait_ge(h_ready, ready + kt + 1)
                        for c in range(2):
                            w = (slice(None), kt, slice(c * P, c * P + P))
                            ins = three(outs[c], w_hi[s % 2][w], w_lo[s % 2][w], b_hi[:, kt], b_lo[:, kt], kt == 0, kt == kk - 1, n)
                            if kt == kk - 1:
                                ins.then_inc(tile_done, 1)
                    return
                for c in range(2):
                    out = tile_slot(t + c, it, tstep)
                    if c == 0:
                        pe.wait_ge(w_hi_done, it * sstep + (s + 1))
                        pe.wait_ge(w_lo_done, it * sstep + (s + 1))
                    for kt in range(kk):
                        w = (slice(None), kt, slice(c * P, c * P + P))
                        ins = three(out, w_hi[s % 2][w], w_lo[s % 2][w], b_hi[:, kt], b_lo[:, kt], kt == 0, kt == kk - 1, n)
                    ins.then_inc(tile_done, 1)

            def use_pm(m):
                if not (isinstance(m, int) and m == 0):
                    pe.wait_ge(pm_free, m)

            def norm(n):
                use_pm(M_NORM[n])
                for kt in range(KT):
                    pe.wait_ge(sq_ready, KT * n + kt + 1)
                    for lo, hi in ((0, HALF), (HALF, TOK)):
                        last = mm(pm[:, at_bank(lo, hi)], ones, tA(kt % 2)[:, lo:hi], start=kt == 0, stop=kt == KT - 1)
                    last.then_inc(sq_used if kt < KT - 1 else pm_done, 1)

            def project_in(l):
                s, t = S_IN[l], T_IN[l]
                slab(s, t, h_hi, h_lo, ready=KT * 2 * l)
                with pe.Fori(0, (4, 2)[l]) as i:
                    for c in range(2):
                        slab(s + 1 + c, t + 2 + 2 * c, h_hi, h_lo, it=i, sstep=2, tstep=4)

            def qk_norm(l):
                if l == 0:
                    pe.wait_ge(mixer_in, 16)
                if l == 1:
                    for g in range(4):
                        pe.wait_ge(pooled, g + 1)
                        use_pm(M_POOL + g)
                        for a, b, x in pieces:
                            at = a + (8 if x == 0 else CTX0 - LAT)
                            last = mm(pm[:, at_bank(a, b)], mx("poolw", g * P, P), tB((g + 1) % 2, PADW)[:, at:at + b - a],
                                      start=True, stop=True)
                        last.then_inc(pm_done, 1)
                for t in (4, 5):
                    taken(pe, T_IN[l] + t)
                use_pm(M_V[l])
                for t in range(TT):
                    last = nc.tensor.transpose(pm[:, t * P:(t + 1) * P], v[:, t * P:(t + 1) * P], ident)
                last.then_inc(pm_done, 1)
                for j in range(5):
                    pe.wait_ge(zsq_ready, 5 * l + j + 1)
                    use_pm(M_VAR[l] + j)
                    for lo, hi in ((0, HALF), (HALF, TOK)):
                        last = mm(pm[:, at_bank(lo, hi)], mx("blk"), tA(j % 2)[:, lo:hi], start=True, stop=True)
                    last.then_inc(pm_done, 1)
                    pe.wait_ge(zn_ready, 5 * l + j + 1)
                    if O_ROT[l] + j:
                        pe.wait_ge(po_free, O_ROT[l] + j)
                    mm(po, mx("rot"), norm_row(j)[:, 0:LAT], start=True, stop=True).then_inc(po_done, 1)

            def attention(l):
                pe.wait_ge(cached_ready, l + 1)
                pe.wait_ge(keys_ready, 2 * l + 2)
                pe.wait_ge(pm_free, M_VAR[l] + 5)

                def max_scores(u, b, i):
                    if b == 0:
                        pe.wait_ge(q_hi_done, i * 4 + 2 * (UNITS * l + u + 1))
                    out, at = tile_slot(T_ATT[l] + 4 * u + b, i, 8), 0
                    for k0, n, mask in attn_blocks(l, u)[b]:
                        last = mm(out[:, at:at + n], qA[u % 2][:, b * P:(b + 1) * P], keysA[u % 2][:, k0:k0 + n],
                                  start=True, stop=mask is None)
                        if mask is not None:
                            last = mm(out[:, at:at + n], ident_r[:], masks_r[:, mask], start=False, stop=True)
                        at += n
                    last.then_inc(tile_done, 1)

                def turn_max(u, i):
                    pe.wait_ge(max_ready, i * 2 + (UNITS * l + u + 1))
                    if l or u:
                        pe.wait_ge(max_in, i * 2 + (UNITS * l + u))
                    for b in range(4):
                        last = mm(prow[0:1, b * P:(b + 1) * P], rowmax_r[:, u % 2, b:b + 1], ident_r[:], start=True, stop=True)
                    last.then_inc(max_turned, 1)

                def scores(u, k, i):
                    t, b0, b1, masks = attn_tiles(l, u)[k]
                    x = key_step(l, u, k)
                    at, keys = slice(b0 * P, b1 * P), slice(t * P, (t + 1) * P)
                    bank = pm[:, x % 2 * 512:x % 2 * 512 + 512]
                    if k >= 2:
                        pe.wait_ge(exp_done, i * 12 + (x - 1))
                    if k == 0:
                        pe.wait_ge(q_lo_done, i * 2 + (UNITS * l + u + 1))
                    mm(bank[:, at], keysA[u % 2][:, keys], qA[u % 2][:, at], start=True, stop=False)
                    if k == 0:
                        pe.wait_ge(max_in, i * 2 + (UNITS * l + u + 1))
                    last = mm(bank[:, at], keysB[u % 2][0:HD + 1, keys], qB[u % 2][0:HD + 1, at], start=False, stop=not masks)
                    for n, (b, m) in enumerate(masks.items()):
                        last = mm(bank[:, b * P:(b + 1) * P], ident_r[:], masks_r[:, m], start=False, stop=n == len(masks) - 1)
                    last.then_inc(scores_done, 1)

                def values(u, k, i):
                    tiles = attn_tiles(l, u)
                    t, b0, b1, _ = tiles[k]
                    x = key_step(l, u, k)
                    if k == 0:
                        pe.wait_ge(po_free, i * 2 + (O_ATT[l] + u))
                        if l == 1:
                            pe.wait_ge(sink_in, i * 2 + (u + 1))
                            mm(po, den_row[HD:HD + 1, u % 2], tA(u % 2, 512)[HD:HD + 1], start=True, stop=False)
                    pe.wait_ge(exp_done, i * 12 + (x + 1))
                    at = slice(b0 * P, b1 * P)
                    mm(po[:, at], vals[u % 2][:, t], probs[x % 3][:, at], start=k == 0 and l == 0, stop=k == len(tiles) - 1
                       ).then_inc(values_done, 1)

                def unit(u, nu, i):
                    n = len(attn_tiles(l, u))
                    for k in range(max(n, 5)):
                        if k < n:
                            scores(u, k, i)
                            if k:
                                values(u, k - 1, i)
                        if nu is not None and 1 <= k <= 4:
                            max_scores(nu, k - 1, i)
                    if nu is not None:
                        turn_max(nu, i)
                    values(u, n - 1, i)

                for b in range(4):
                    max_scores(0, b, 0)
                turn_max(0, 0)
                units(pe, unit)

            def project_out(l):
                pe.wait_ge(out_kept, (UNITS + 2) * (l + 1))
                if l == 0:
                    pe.wait_ge(prod_lo, P_FFN)
                else:
                    pe.wait_ge(pm_free, M_NORM[3])
                with pe.Fori(0, 2) as i:
                    for c in range(2):
                        slab(S_OUT[l] + c, T_OUT[l] + 2 * c, mix_hi, mix_lo, it=i, sstep=2, tstep=4)

            def ffn():
                s, t, p = S_FFN, T_FFN, P_FFN
                for n, hidden in enumerate(FFN_PARTS):
                    if n == 0:
                        slab(s, t, h_hi, h_lo, ready=KT)
                        slab(s + 1, t + 2, h_hi, h_lo)
                    with pe.Fori(int(n == 0), hidden // 2) as i:
                        for c in range(2):
                            slab(s + c, t + 2 * c, h_hi, h_lo, it=i, sstep=2, tstep=4)
                    s, t, p = s + hidden, t + 2 * hidden, p + hidden
                    pe.wait_ge(prod_lo, p)
                    with pe.Fori(0, 2) as i:
                        for c in range(2):
                            slab(s + c, t + 2 * c, fh_hi, fh_lo, kk=hidden, it=i, sstep=2, tstep=4)
                    s, t = s + 4, t + 8

            def routing():
                pe.wait_ge(h_ready, 4 * KT)
                pe.wait_ge(rw_ready, 1)
                use_pm(M_LOGIT)
                for t in range(TT):
                    for kt in range(KT):
                        a = (slice(None), kt, slice(t * P, t * P + P))
                        r = slice(kt * NE, kt * NE + NE)
                        last = three(pm[:, t * NE:(t + 1) * NE], h_hi[a], h_lo[a], rw_hi[:, r], rw_lo[:, r], kt == 0, kt == KT - 1, NE)
                last.then_inc(pm_done, 1)
                for n in range(2 * TT):
                    out = tile_slot(T_TOK + n, 0, 0)
                    src = h_hi if n < TT else h_lo
                    t = n % TT
                    for kt in range(KT):
                        last = nc.tensor.transpose(out[:, kt * P:(kt + 1) * P], src[:, kt, t * P:(t + 1) * P].bitcast(F32), ident)
                    last.then_inc(tile_done, 1)
                pe.wait_ge(mask_ready, 1)
                use_pm(M_RANK)
                mask = rt[:, 11, :]
                for t in range(TT):
                    for u in range(t + 1):
                        mm(pm[:, t * NE:(t + 1) * NE], ro("upper") if u == t else ones, mask[:, u * NE:(u + 1) * NE],
                           start=u == 0, stop=u == t)
                for t in range(TT):
                    last = mm(pm[:, TT * NE:(TT + 1) * NE], ones, mask[:, t * NE:(t + 1) * NE], start=t == 0, stop=t == TT - 1)
                last.then_inc(pm_done, 1)

            def experts():
                n_items = items(pe)

                def gather(kt, t, j, step):
                    out = tile_slot(t, j, step)
                    for x, src in enumerate((tok_hi, tok_lo)):
                        for u in range(TT):
                            last = mm(out[:, x * CAP:(x + 1) * CAP], src[:, u, kt * P:(kt + 1) * P], onehot[:, u, :],
                                      start=u == 0, stop=u == TT - 1)
                    last.then_inc(tile_done, 1)

                def slots(j):
                    if isinstance(j, int):
                        pe.wait_ge(pm_free, M_MOE)
                    else:
                        pe.wait_ge(slots_kept, j)
                    turned = [pm[:, t * P:(t + 1) * P] for t in range(TT)]
                    turned += [prow[:, t * P:(t + 1) * P] for t in range(4)] + [po[:, P:2 * P]]
                    for n, out in enumerate(turned):
                        sl, t = divmod(n, TT)
                        nc.tensor.transpose(out, onehot[:, t, sl * P:(sl + 1) * P].bitcast(F32), ident)
                    for sl in range(2):
                        for t in range(TT):
                            last = mm(po[:, sl:sl + 1], onehot[:, t, sl * P:(sl + 1) * P].bitcast(F32),
                                      item_gate[:, t, bass.ds(j, 1)], start=t == 0, stop=t == TT - 1)
                    last.then_inc(slots_turned, 1)

                for t in (2, 1):
                    taken(pe, T_MOE - t)
                pe.wait_ge(onehot_ready, 1)
                for kt in range(KT):
                    gather(kt, T_MOE + kt, 0, 0)
                slots(0)
                with pe.Fori(0, n_items) as j:
                    T = T_ITEM
                    with pe.Fori(0, 4) as i:
                        pe.wait_ge(tile_free[0], j * (ITEM_TILES // 2) + T // 2)
                        pe.wait_ge(tile_free[1], j * (ITEM_TILES // 2) + T // 2)
                        for w in range(2):
                            for c in range(2):
                                t = T + 2 * w + c
                                pe.wait_ge(tile_free[t % 2], j * (ITEM_TILES // 2) + i * 2 + t // 2)
                                if c == 0:
                                    pe.wait_ge(w_hi_done, j * ITEM_SLABS + i * 2 + (S_MOE + w + 1))
                                    pe.wait_ge(w_lo_done, j * ITEM_SLABS + i * 2 + (S_MOE + w + 1))
                                for kt in range(KT):
                                    a = (slice(None), kt, slice(c * P, c * P + P))
                                    last = three(pp[t % 2], w_hi[w][a], w_lo[w][a], g_hl[:, kt, 0], g_hl[:, kt, 1], kt == 0, kt == KT - 1, CAP)
                                last.then_inc(tile_done, 1)

                    def outputs(n):
                        for sl in range(2):
                            out = tile_slot(T + OUT_AT[n] + sl, j, ITEM_TILES)
                            if sl == 0:
                                pe.wait_ge(w_hi_done, j * ITEM_SLABS + (S_MOE + 8 + n + 1))
                                pe.wait_ge(w_lo_done, j * ITEM_SLABS + (S_MOE + 8 + n + 1))
                            for f in range(8):
                                a = (slice(None), f, slice(sl * P, sl * P + P))
                                last = three(out, e_hi[a], e_lo[a], w_hi[n % 2][:, f], w_lo[n % 2][:, f], f == 0, f == 7, SLAB)
                            last.then_inc(tile_done, 1)

                    def next_tokens(*tiles):
                        for kt in tiles:
                            gather(kt, T + GATHER_AT[kt], j, ITEM_TILES)

                    pe.wait_ge(onehot_ready, j + 2)
                    next_tokens(0, 1)
                    pe.wait_ge(prod_lo, j * 8 + (P_MOE + 8))
                    outputs(0)
                    next_tokens(2, 3)
                    outputs(1)
                    outputs(2)
                    next_tokens(4, 5)
                    outputs(3)
                    next_tokens(6, 7)
                    for sl in range(2):
                        pe.wait_ge(tile_free[sl], j * (ITEM_TILES // 2) + (T + OUT_AT[3]) // 2 + 1)
                    pe.wait_ge(slots_kept, j + 1)
                    for d in range(KT):
                        out = tile_slot(T + COMBINE_AT + d, j, ITEM_TILES)
                        for sl in range(2):
                            for y in (y_hi, y_lo):
                                for lo, hi in ((0, HALF), (HALF, TOK)):
                                    last = mm(out[:, at_bank(lo, hi)], y[:, sl, d * P:(d + 1) * P], selT[:, sl, lo:hi],
                                              start=sl == 0 and y is y_hi, stop=sl == 1 and y is y_lo)
                        last.then_inc(tile_done, 1)
                    slots(j + 1)

            norm(0)
            project_in(0)
            qk_norm(0)
            attention(0)
            project_out(0)
            norm(1)
            ffn()
            norm(2)
            project_in(1)
            qk_norm(1)
            attention(1)
            project_out(1)
            norm(3)
            routing()
            experts()

        @block.scalar
        def _(act):
            A = nc.scalar.activation

            def hi(s, it=0, step=0, tstep=0):
                act.wait_ge(slab_in[s % 2], half(s, it, step) * 16 + 16)
                if s >= 2:
                    act.wait_ge(tile_done, it * tstep + tiles_after(s - 2))
                A(w_hi[s % 2][:], raw[s % 2][:], ACT.Copy).then_inc(w_hi_done, 1)

            def norm(n):
                l, second = divmod(n, 2)
                if n == 0:
                    act.wait_ge(x_in, 16)
                for kt in range(KT):
                    if n:
                        taken(act, (T_OUT[0], T_IN[1] - KT, T_OUT[1])[n - 1] + kt)
                    if kt >= 2:
                        act.wait_ge(sq_used, (KT - 1) * n + kt - 1)
                    A(tA(kt % 2), xT[:, kt], ACT.Square, scale=D ** -0.5).then_inc(sq_ready, 1)
                act.wait_ge(pm_done, M_NORM[n] + 1)
                A(two(tB(0)), banks(pm), ACT.Sqrt, bias=eps[:]).then_inc(pm_free, 1)
                for kt in range(KT):
                    act.wait_ge(scaled, KT * n + kt + 1)
                    for x, (a, b) in enumerate(((0, LAT), (LAT, TOK))):
                        last = A(h_hi[:, kt, a:b], tA(kt % 2)[:, a:b], ACT.Identity, bias=modv[:, NMOD * l + 24 * second + kt, x:x + 1])
                    last.then_inc(h_hi_done, 1)

            def copy_tile(t, dst):
                act.wait_ge(tile_done, t + 1)
                A(two(dst), banks(pp[t % 2]), ACT.Copy).then_inc(tile_free[t % 2], 1)

            def project_in(l):
                s, t = S_IN[l], T_IN[l]
                for n in range(3):
                    hi(s + 1)
                    for c in range(2):
                        j = 2 * n + c
                        copy_tile(t + c, q[:, j] if j < 4 else (k, v)[j - 4][:])
                    s, t = s + 1, t + 2
                if l == 0:
                    for n in range(2):
                        hi(s + 1)
                        for c in range(2):
                            copy_tile(t + c, tA(c))
                        hi(s + 2)
                        hi(s + 3)
                        for c in range(2):
                            taken(act, t + 4 + c)
                            A(mix_hi[:, 4 + 2 * n + c], tB(c), ACT.Copy).then_inc(prod_hi, 1)
                        s, t = s + 3, t + 6
                else:
                    act.wait_ge(pads_zero, 2)
                    for n in range(2):
                        hi(s + 1)
                        for c in range(2):
                            g = 2 * n + c
                            if g >= 2:
                                act.wait_ge(pooled, g - 1)
                            act.wait_ge(tile_done, t + c + 1)
                            for a, b, x in pieces:
                                at = a + (8 if x == 0 else CTX0 - LAT)
                                ins = A(tA(c, PADW)[:, at:at + b - a], pp[(t + c) % 2][:, at_bank(a, b)], ACT.Copy)
                            ins.then_inc(tile_free[(t + c) % 2], 1)
                        s, t = s + 1, t + 2

            def qk_norm(l):
                if l == 1:
                    for g in range(4):
                        act.wait_ge(pm_done, M_POOL + g + 1)
                        A(two(mix_hi[:, 4 + g]), banks(pm), ACT.Copy, scale=kp("pscale", g, 1)).then_inc(pool_hi, 1)
                act.wait_ge(pm_done, M_V[l] + 1)
                for g in range(2):
                    rows, _ = unit_rows(g)
                    last = A(vals[g][:, PAST // P:, rows], pm[:, 0:TOK].rearrange("p (t n) -> p t n", n=P)[:, :, rows], ACT.Copy)
                last.then_inc(pm_free, 1)

                def square(j):
                    A(tA(j % 2), norm_row(j), ACT.Square, scale=HD ** -0.5).then_inc(zsq_ready, 1)

                act.wait_ge(*((prod_lo, P_FFN), (pooled, 4))[l])
                square(0)
                for j in range(5):
                    if j < 4:
                        square(j + 1)
                    act.wait_ge(pm_done, M_VAR[l] + j + 1)
                    if j >= 2:
                        act.wait_ge(zn_ready, 5 * l + j)
                        act.wait_ge(rotated, 5 * l + j - 1)
                    A(two(tB(j % 2)), banks(pm), ACT.Sqrt, bias=eps[:]).then_inc(pm_free, 1)
                    if j == 2:
                        act.wait_ge(rotated, 5 * l + 1)
                        for g in range(2):
                            rows, _ = unit_rows(g)
                            A(keysA[g][rows, PAST:KEYS], k[rows], ACT.Copy).then_inc(k_hi_done, 1)
                            last = A(keysB[g][0:HD, PAST:KEYS], k[rows], ACT.Copy)
                        last.then_inc(keys_ready, 1)
                act.dma_start(newk_d[l], k[:, LAT:TOK]).then_inc(kv_out, 16)
                act.dma_start(newv_d[l], v[:, LAT:TOK]).then_inc(kv_out, 16)

            def attention(l):
                act.wait_ge(rotated, 5 * l + 5)

                def q_hi(u, i):
                    for half_rows in (slice(0, HD), slice(HD, P)):
                        A(blocks(qA[u % 2][half_rows]), unit_q(u, i), ACT.Copy).then_inc(q_hi_done, 1)

                def max_row(u, i):
                    act.wait_ge(max_turned, i * 2 + (UNITS * l + u + 1))
                    row = qB[u % 2][HD:HD + 1]
                    A(row, prow[0:1, :], ACT.Copy).then_inc(max_in, 1)
                    if l == 1:
                        act.wait_ge(max_in, i * 2 + (UNITS * l + u + 1))
                        parts = 4 if u >= CTX_UNITS else 1
                        for b in range(parts):
                            at = slice(b * 512 // parts, (b + 1) * 512 // parts)
                            last = A(tA(u % 2, 512)[HD:HD + 1, at], row[:, at].bitcast(F32), ACT.Exp,
                                     bias=sinkcur[HD:HD + 1, u % 2, b:b + 1], scale=-SCALE)
                        last.then_inc(sink_in, 1)

                def exps(u, k, i):
                    _, b0, b1, _ = attn_tiles(l, u)[k]
                    x = key_step(l, u, k)
                    act.wait_ge(scores_done, i * 12 + (x + 1))
                    if x >= 3 and k >= 3:
                        act.wait_ge(values_done, i * 12 + (x - 2))
                    A(probs[x % 3][:, b0 * P:b1 * P], pm[:, x % 2 * 512 + b0 * P:x % 2 * 512 + b1 * P], ACT.Exp, scale=SCALE
                      ).then_inc(exp_done, 1)

                def unit(u, nu, i):
                    for k in range(len(attn_tiles(l, u))):
                        exps(u, k, i)
                        if nu is not None and k == 0:
                            q_hi(nu, i)
                    if nu is not None:
                        max_row(nu, i)

                q_hi(0, 0)
                max_row(0, 0)
                units(act, unit)

            def ffn():
                act.wait_ge(kv_out, 32)
                s, t, p = S_FFN, T_FFN, P_FFN
                for hidden in FFN_PARTS:
                    hi(s + 1)
                    with act.Fori(0, hidden // 2) as i:
                        for c in range(2):
                            act.wait_ge(tile_done, i * 4 + (t + c + 1))
                            A(two(tA(c)), banks(pp[(t + c) % 2]), ACT.Silu).then_inc(tile_free[(t + c) % 2], 1)
                        hi(s + 2, i, 2, 4)
                        for c in range(2):
                            taken(act, t + 2 + c, i, 4)
                            A(fh_hi[:, bass.ds(i * 2 + c, 1)], tB(c).unsqueeze(1), ACT.Copy).then_inc(prod_hi, 1)
                        hi(s + 3, i, 2, 4)
                    s, t, p = s + hidden, t + 2 * hidden, p + hidden
                    for n in range(1, 4):
                        hi(s + n + 1)
                    s, t = s + 4, t + 8

            def routing():
                act.wait_ge(route_in, 16)
                A(rw_hi[:], ro("router"), ACT.Copy).then_inc(rw_hi_done, 1)
                act.wait_ge(kv_out, 64)
                for n in range(0, 2 * TT, 2):
                    act.wait_ge(tile_done, T_TOK + n + 1)
                    dst = (tok_hi if n < TT else tok_lo)[:, n % TT]
                    A(dst, pp[n % 2][:, :], ACT.Copy).then_inc(tile_free[n % 2], 1)
                act.wait_ge(gap_ready, 1)
                A(rc[:, 5, 0:TT], rc[:, 4, 0:TT], ACT.Exp).then_inc(gap_exp, 1)

            def experts():
                n_items = items(act)

                def hi_item(c, j, done, i=0):
                    act.wait_ge(slab_in[c % 2], j * (8 * ITEM_SLABS) + i * 16 + 16 * ((S_MOE + c) // 2 + 1))
                    act.wait_ge(tile_done, done)
                    A(w_hi[c % 2][:], raw[c % 2][:], ACT.Copy).then_inc(w_hi_done, 1)

                def slots(j):
                    act.wait_ge(slots_turned, j + 1)
                    A(gslot[:], po[:, 0:2], ACT.Copy)
                    A(selT[:, 0], pm[:, 0:TOK], ACT.Copy)
                    A(selT[:, 1, 0:512], prow, ACT.Copy)
                    A(selT[:, 1, 512:TOK], po[:, P:2 * P], ACT.Copy).then_inc(slots_kept, 1)

                slots(0)
                hi_item(1, 0, T_ITEM)
                with act.Fori(0, n_items) as j:
                    t = T_ITEM
                    with act.Fori(0, 4) as i:
                        for c in range(2):
                            act.wait_ge(tile_done, j * ITEM_TILES + i * 4 + (t + c + 1))
                            A(tA(c, CAP), pp[(t + c) % 2][:, 0:CAP], ACT.Silu).then_inc(tile_free[(t + c) % 2], 1)
                        hi_item(2, j, j * ITEM_TILES + i * 4 + (t + 2), i)
                        for c in range(2):
                            act.wait_ge(tile_free[c], j * (ITEM_TILES // 2) + i * 2 + ((t + 2) // 2 + 1))
                            A(e_hi[:, bass.ds(i * 2 + c, 1)], tB(c, CAP).unsqueeze(1), ACT.Copy).then_inc(prod_hi, 1)
                        hi_item(3, j, j * ITEM_TILES + i * 4 + (t + 4), i)
                    for n in range(4):
                        for sl in range(2):
                            act.wait_ge(tile_done, j * ITEM_TILES + (t + OUT_AT[n] + sl + 1))
                            A(y_hi[:, sl, n * SLAB:(n + 1) * SLAB], pp[sl][:, 0:SLAB], ACT.Copy, scale=gslot[:, sl:sl + 1]
                              ).then_inc(yhi_done, 1)
                        hi_item(10 + n, j, j * ITEM_TILES + (t + OUT_AT[n] + 2))
                    slots(j + 1)

            act.wait_ge(eps_set, 1)
            act.wait_ge(kept_in, 16)
            act.wait_ge(cond_in, 16)
            A(scond[:], scond[:], ACT.Silu).then_inc(cond_ready, 1)
            hi(0)
            norm(0)
            project_in(0)
            qk_norm(0)
            attention(0)
            for n in range(4):
                hi(S_OUT[0] + n + 1)
            norm(1)
            ffn()
            norm(2)
            project_in(1)
            qk_norm(1)
            attention(1)
            for n in range(4):
                hi(S_OUT[1] + n + 1)
            norm(3)
            routing()
            experts()

        @block.vector
        def _(dve):
            V = nc.vector
            steps, kept_mods = [0], [0]

            def step(ins):
                steps[0] += 1
                ins.then_inc(dve_step, 1)
                dve.wait_ge(dve_step, steps[0])

            def lo(s, it=0, sstep=0):
                dve.wait_ge(w_hi_done, it * sstep + (s + 1))
                V.tensor_tensor(w_lo[s % 2][:], raw[s % 2][:], w_hi[s % 2][:].bitcast(F32), ALU.subtract).then_inc(w_lo_done, 1)

            def first_mods():
                dve.wait_ge(cond_ready, 1)
                for n in range(MOD_FIRST):
                    if n % 4 == 0:
                        dve.wait_ge(mod_first_in[n // 4], 16)
                    dot(mod_first[n // 8][:, n % 8], n, 0)

            def dot(w, n, at):
                for x in range(2):
                    if n or x:
                        dve.wait_ge(mod_used, at * 2 + (2 * n + x))
                    V.scalar_tensor_tensor(mod_prod[:], w, 1.0, scond[:, x], ALU.mult, ALU.mult,
                                           accum_out=modv[:, bass.ds(at + n, 1), x:x + 1].rearrange("p a c -> p (a c)")
                                           ).then_inc(mod_used, 1)

            def mods(n0, count, it=0, step=0):
                for c in range(count):
                    n = n0 + c
                    dve.wait_ge(mod_in[n % 2], it * (16 * step // 2) + 16 * ((n - MOD_FIRST) // 2 + 1))
                    dot(modraw[n % 2][:], n, it * step)

            def keep_mods(n0, n):
                kept_mods[0] += 1
                dve.wait_ge(mod_used, 2 * (n0 + n))
                V.tensor_tensor(modv[:, n0:n0 + n], modv[:, n0:n0 + n],
                                kp("bmod", n0, n).unsqueeze(2).to_broadcast([P, n, 2]), ALU.add).then_inc(mod_kept, 1)
                dve.wait_ge(mod_kept, kept_mods[0])

            def norm(n):
                l, second = divmod(n, 2)
                sh = NMOD * l + 24 * second
                step(V.scalar_tensor_tensor(gainA[:], modv[:, sh + 8:sh + 16], 1.0,
                                            kp(("norm1", "norm2")[second], KT * l, KT).unsqueeze(2).to_broadcast([P, KT, 2]),
                                            ALU.add, ALU.mult))
                dve.wait_ge(pm_free, M_NORM[n] + 1)
                step(V.reciprocal(tB(0), tB(0)))

                def scale(kt):
                    if kt >= 2:
                        dve.wait_ge(h_ready, KT * n + kt - 1)
                    for x, (a, b) in enumerate(((0, LAT), (LAT, TOK))):
                        last = V.scalar_tensor_tensor(tA(kt % 2)[:, a:b], xT[:, kt, a:b], gainA[:, kt, x:x + 1], tB(0)[:, a:b],
                                                      ALU.mult, ALU.mult)
                    last.then_inc(scaled, 1)

                scale(0)
                for kt in range(KT):
                    if kt < KT - 1:
                        scale(kt + 1)
                    dve.wait_ge(h_hi_done, KT * n + kt + 1)
                    for x, (a, b) in enumerate(((0, LAT), (LAT, TOK))):
                        last = V.scalar_tensor_tensor(h_lo[:, kt, a:b], tA(kt % 2)[:, a:b], modv[:, sh + kt, x:x + 1],
                                                      h_hi[:, kt, a:b].bitcast(F32), ALU.add, ALU.subtract)
                    last.then_inc(h_ready, 1)

            def conv(n):
                s, t = S_IN[0] + 3 + 3 * n, T_IN[0] + 6 + 6 * n
                m = 22 + 5 * n
                lo(s + 1)
                mods(m, 2)
                lo(s + 2)
                mods(m + 2, 1)
                for c in range(2):
                    taken(dve, t + c)
                    dve.wait_ge(tile_done, t + 2 + c + 1)
                    V.tensor_tensor(two(tB(c)), banks(pp[(t + c) % 2]), two(tA(c)), ALU.mult).then_inc(tile_free[(t + c) % 2], 1)
                lo(s + 3)
                mods(m + 3, 2)
                for c in range(2):
                    u, y, g = tB(c), tA(c), 2 * n + c
                    taken(dve, t + 2 + c)
                    w = [kp("conv", 4 * x + g, 1) for x in range(3)]
                    step(V.tensor_scalar(y, u, w[1], None, ALU.mult))
                    for a, b in ((0, LAT), (LAT, TOK)):
                        step(V.scalar_tensor_tensor(y[:, a + 1:b], u[:, a:b - 1], w[0], y[:, a + 1:b], ALU.mult, ALU.add))
                        step(V.scalar_tensor_tensor(y[:, a:b - 1], u[:, a + 1:b], w[2], y[:, a:b - 1], ALU.mult, ALU.add))
                    dve.wait_ge(tile_done, t + 4 + c + 1)
                    V.tensor_tensor(two(tB(c)), banks(pp[(t + c) % 2]), two(y), ALU.mult).then_inc(tile_free[(t + c) % 2], 1)
                for c in range(2):
                    g = 2 * n + c
                    dve.wait_ge(prod_hi, g + 1)
                    V.tensor_tensor(mix_lo[:, 4 + g], tB(c), mix_hi[:, 4 + g].bitcast(F32), ALU.subtract).then_inc(prod_lo, 1)

            def pool_tile(g):
                x, w = tA(g % 2, PADW), 2 << g
                if g:
                    dve.wait_ge(pm_done, M_POOL + g)
                taken(dve, T_IN[1] + 6 + g)
                src, r, lo_, hi_ = x, 0, 0, PADW
                for m in range(g + 1):
                    dst = tB(m % 2, PADW)
                    a, b = (1, 0) if m == 0 else (2 ** (m - 1), 2 ** (m - 1))
                    lo_, hi_ = lo_ + a, hi_ - b
                    step(V.tensor_tensor(dst[:, lo_:hi_], src[:, lo_ - a:hi_ - a], src[:, lo_ + b:hi_ + b], ALU.add))
                    src = dst
                for x0, n in ((8, LAT), (CTX0, CTX)):
                    for side, at in enumerate((x0, x0 + n - 8)):
                        step(V.tensor_tensor(src[:, at:at + 8], src[:, at:at + 8], kp("edge", 16 * g + 8 * side, 8), ALU.mult))
                out = tB((g + 1) % 2, PADW)
                V.scalar_tensor_tensor(out[:, 8:CTX0 + CTX], src[:, 8:CTX0 + CTX], 1.0 / w, x[:, 8:CTX0 + CTX], ALU.mult,
                                       ALU.subtract).then_inc(pooled, 1)

            def pool_lo(g):
                dve.wait_ge(pool_hi, g + 1)
                V.scalar_tensor_tensor(two(mix_lo[:, 4 + g]), banks(pm), kp("pscale", g, 1), two(mix_hi[:, 4 + g].bitcast(F32)),
                                       ALU.mult, ALU.subtract).then_inc(pm_free, 1)

            def project_in(l):
                for n in range(3):
                    lo(S_IN[l] + n + 1)
                    if l == 0:
                        mods(MOD_FIRST + 2 * n, 2)
                if l == 0:
                    for n in range(2):
                        conv(n)
                    return
                step(V.memset(tmpB[:], 0.0))
                V.memset(tA(0, PADW), 0.0).then_inc(pads_zero, 1)
                V.memset(tA(1, PADW), 0.0).then_inc(pads_zero, 1)
                for n in range(2):
                    lo(S_IN[l] + 4 + n)
                for g in range(5):
                    if g < 4:
                        pool_tile(g)
                    if g:
                        pool_lo(g - 1)

            def qk_norm(l):
                dve.wait_ge(mixer_in, 16)
                for j in range(5):
                    z, r = norm_row(j), tB(j % 2)
                    dve.wait_ge(pm_free, M_VAR[l] + j + 1)
                    step(V.reciprocal(r, r))
                    V.scalar_tensor_tensor(z, z, kp("gain", 2 * l + (j == 0), 1), r, ALU.mult, ALU.mult).then_inc(zn_ready, 1)
                    dve.wait_ge(po_done, 5 * l + j + 1)
                    V.tensor_tensor(r[:, 0:LAT], po, mx("sin"), ALU.mult).then_inc(po_free, 1)
                    step(V.tensor_tensor(z[:, 0:LAT], z[:, 0:LAT], mx("cos"), ALU.mult))
                    dve.wait_ge(po_free, O_ROT[l] + j + 1)
                    V.tensor_tensor(z[:, 0:LAT], z[:, 0:LAT], r[:, 0:LAT], ALU.add).then_inc(rotated, 1)
                    if j == 3:
                        for g in range(2):
                            rows, others = unit_rows(g)
                            dve.wait_ge(k_hi_done, 2 * l + g + 1)
                            last = V.tensor_tensor(keysA[g][others, PAST:KEYS], k[rows], keysA[g][rows, PAST:KEYS].bitcast(F32), ALU.subtract)
                        last.then_inc(keys_ready, 1)

            def attention(l):
                dve.wait_ge(rotated, 5 * l + 5)

                def q_lo(u, i):
                    rows, _ = unit_rows(u)
                    dve.wait_ge(q_hi_done, i * 4 + 2 * (UNITS * l + u + 1))
                    V.tensor_tensor(blocks(qB[u % 2][0:HD]), unit_q(u, i), blocks(qA[u % 2][rows]).bitcast(F32), ALU.subtract
                                    ).then_inc(q_lo_done, 1)

                def maxima(u, i):
                    for b in range(4):
                        t = T_ATT[l] + 4 * u + b
                        n = sum(x[1] for x in attn_blocks(l, u)[b])
                        dve.wait_ge(tile_done, i * 8 + (t + 1))
                        V.tensor_reduce(rowmax[:, u % 2, b:b + 1], pp[t % 2][:, 0:n], AX, ALU.max).then_inc(tile_free[t % 2], 1)
                    for b in (2, 3):
                        taken(dve, T_ATT[l] + 4 * u + b, i, 8)
                    if l == 0:
                        V.tensor_copy(rowmax_r[:, u % 2], rowmax[:, u % 2]).then_inc(max_ready, 1)
                        return
                    for sink, to in ((kp("sink"), None), (sink8, 1)):
                        col = sink[:, head(u, i)]
                        if u < CTX_UNITS:
                            col = col.to_broadcast([P, 4])
                        if to is None:
                            V.tensor_copy(sinkcur[:, u % 2], col)
                        else:
                            V.tensor_tensor(rowmax_r[:, u % 2], rowmax[:, u % 2], col, ALU.max).then_inc(max_ready, 1)

                def out(u, i):
                    rows, others = unit_rows(u)
                    last = key_step(l, u, len(attn_tiles(l, u)) - 1)
                    dve.wait_ge(values_done, i * 12 + (last + 1))
                    V.reciprocal(tB(1, 512)[rows], po[others]).then_inc(inverse_done, 1)
                    dve.wait_ge(inverse_done, i * 2 + (UNITS * l + u + 1))
                    dve.wait_ge(out_kept, i * 2 + ((UNITS + 2) * l + u + 1))
                    V.tensor_tensor(att_out(u), po[rows], tB(1, 512)[rows], ALU.mult).then_inc(po_free, 1)

                def unit(u, nu, i):
                    if nu is not None:
                        q_lo(nu, i)
                        maxima(nu, i)
                    out(u, i)

                q_lo(0, 0)
                maxima(0, 0)
                units(dve, unit)

            def add_tile(t, d, gate, it=0, tstep=0, dyn=None):
                dve.wait_ge(tile_done, it * tstep + (t + 1))
                for a, b, x in pieces:
                    last = V.scalar_tensor_tensor(xT[:, d, a:b], pp[t % 2][:, at_bank(a, b)], modv[:, gate + d, x:x + 1], xT[:, d, a:b],
                                                  ALU.mult, ALU.add)
                last.then_inc(tile_free[t % 2], 1)

            def project_out(l):
                dve.wait_ge(po_free, O_ATT[l] + UNITS)
                for n in range(4):
                    s = S_OUT[l] + n
                    lo(s + 1)
                    if l == 0:
                        mods(32 + 2 * n, 2)
                    for c in range(2):
                        add_tile(T_OUT[l] + 2 * n + c, 2 * n + c, NMOD * l + 16)

            def ffn():
                s, t, p, m = S_FFN, T_FFN, P_FFN, 40
                for part, hidden in enumerate(FFN_PARTS):
                    spare = 1 if part == 0 else 2
                    with dve.Fori(0, hidden // 2) as i:
                        lo(s + 1, i, 2)
                        mods(m, spare, i, 2 * spare)
                        lo(s + 2, i, 2)
                        mods(m + spare, spare, i, 2 * spare)
                        for c in range(2):
                            taken(dve, t + c, i, 4)
                            dve.wait_ge(tile_done, i * 4 + (t + 2 + c + 1))
                            V.tensor_tensor(two(tB(c)), banks(pp[(t + c) % 2]), two(tA(c)), ALU.mult).then_inc(tile_free[(t + c) % 2], 1)
                        for c in range(2):
                            dve.wait_ge(prod_hi, i * 2 + (p + c + 1))
                            at = (slice(None), bass.ds(i * 2 + c, 1))
                            V.tensor_tensor(fh_lo[at], tB(c).unsqueeze(1), fh_hi[at].bitcast(F32), ALU.subtract).then_inc(prod_lo, 1)
                    s, t, p, m = s + hidden, t + 2 * hidden, p + hidden, m + spare * hidden
                    if part == 0:
                        keep_mods(40, 8)
                    spare = 1 if part == 2 else 2
                    for n in range(4):
                        lo(s + 1)
                        mods(m, spare)
                        for c in range(2):
                            add_tile(t + c, 2 * n + c, 40)
                        s, t, m = s + 1, t + 2, m + spare

            def routing():
                dve.wait_ge(rw_hi_done, 1)
                V.tensor_tensor(rw_lo[:], ro("router"), rw_hi[:].bitcast(F32), ALU.subtract).then_inc(rw_ready, 1)

                def row(i):
                    return rt[:, i].rearrange("p (t e) -> p t e", e=NE)

                def col(i):
                    return rc[:, i, 0:TT]

                def wide(a):
                    return a.unsqueeze(2).to_broadcast([P, TT, NE])

                def every(a, n=TT):
                    return a.unsqueeze(1).to_broadcast([P, n, a.shape[-1]])

                dve.wait_ge(pm_done, M_LOGIT + 1)
                ins = V.tensor_tensor(row(0), pm[:, 0:TT * NE].rearrange("p (t e) -> p t e", e=NE), every(kp("rbias")), ALU.add)
                ins.then_inc(pm_free, 1)
                dve.wait_ge(pm_free, M_LOGIT + 1)
                for n in range(1, 2 * TT, 2):
                    dve.wait_ge(tile_done, T_TOK + n + 1)
                    V.tensor_copy((tok_hi if n < TT else tok_lo)[:, n % TT], pp[n % 2][:, :]).then_inc(tile_free[n % 2], 1)
                for x in range(2):
                    step(V.tensor_reduce(col(x), row(0), AX, ALU.max))
                    step(V.tensor_tensor(row(1), row(0), wide(col(x)), ALU.is_equal))
                    step(V.tensor_tensor(row(1), row(1), every(ro("desc")), ALU.mult))
                    step(V.tensor_reduce(col(2), row(1), AX, ALU.max))
                    step(V.tensor_tensor(row(2 + x), row(1), wide(col(2)), ALU.is_equal))
                    if x == 0:
                        step(V.scalar_tensor_tensor(row(0), row(2), NEG, row(0), ALU.mult, ALU.add))
                V.tensor_tensor(col(4), col(1), col(0), ALU.subtract).then_inc(gap_ready, 1)
                V.tensor_tensor(row(11), row(2), row(3), ALU.add).then_inc(mask_ready, 1)
                dve.wait_ge(mask_ready, 1)
                dve.wait_ge(gap_exp, 1)
                step(V.tensor_scalar(col(3), col(5), 1.0, None, ALU.add))
                step(V.reciprocal(col(0), col(3)))
                step(V.tensor_tensor(col(1), col(5), col(0), ALU.mult))
                step(V.tensor_tensor(row(4), row(2), wide(col(0)), ALU.mult))
                step(V.tensor_tensor(row(5), row(3), wide(col(1)), ALU.mult))
                step(V.tensor_tensor(row(4), row(4), row(5), ALU.add))
                dve.wait_ge(pm_done, M_RANK + 1)
                step(V.tensor_copy(rt[:, 6], pm[:, 0:TT * NE]))
                ins = V.tensor_copy(rt[:, 7, 0:NE], pm[:, TT * NE:(TT + 1) * NE])
                ins.then_inc(pm_free, 1)
                dve.wait_ge(pm_free, M_RANK + 1)
                step(V.scalar_tensor_tensor(row(8), row(6), 1.0, row(11), ALU.add, ALU.mult))
                for r in range(ROUNDS):
                    step(V.tensor_scalar(rcand[:, :, r * NE:(r + 1) * NE], row(8), -1.0 - CAP * r, None, ALU.add))
                flag, rank = rc[:, 0], rc[:, 1]
                step(V.tensor_tensor(flag.rearrange("p (r e) -> p r e", e=NE), every(rt[:, 7, 0:NE], ROUNDS),
                                     ro("thr").rearrange("p (r e) -> p r e", e=NE), ALU.is_gt))
                big = rbig[:, 0:NCAND * NCAND].rearrange("p (a b) -> p a b", b=NCAND)
                step(V.tensor_tensor(big, ro("u24").rearrange("p (a b) -> p a b", b=NCAND), every(flag, NCAND), ALU.mult))
                step(V.tensor_reduce(rank, big, AX, ALU.add))
                step(V.tensor_tensor(rsel[:], every(rank, ROOM), ro("jidx").rearrange("p (j i) -> p j i", i=NCAND), ALU.is_equal))
                step(V.tensor_tensor(rsel[:], rsel[:], every(flag, ROOM), ALU.mult))
                small = rbig[:, 0:ROOM * NCAND].rearrange("p (j i) -> p j i", i=NCAND)
                step(V.tensor_tensor(small, rsel[:], every(ro("cand"), ROOM), ALU.mult))
                step(V.tensor_reduce(rc[:, 2, 0:ROOM], small, AX, ALU.add))
                step(V.tensor_reduce(rc[:, 2, ROOM:ROOM + 1], flag, AX, ALU.add))
                step(V.tensor_copy(item_no[:], rc[:, 2, 0:ROOM + 1]))
                big = rbig[:].rearrange("p (t j i) -> p t j i", t=TT, j=ROOM)

                def per_item(out):
                    for t in range(TT):
                        last = V.tensor_tensor(big[:, t], rsel[:], every(rcand[:, t], ROOM), ALU.mult)
                    step(last)
                    return V.tensor_reduce(out[:], big, AX, ALU.add)

                step(per_item(item_pos))
                for r in range(ROUNDS):
                    last = V.tensor_copy(rcand[:, :, r * NE:(r + 1) * NE], row(4))
                step(last)
                per_item(item_gate).then_inc(routed, 1)
                dve.wait_ge(iota_in, 16)

            def experts():
                n_items = items(dve)

                def lo_item(c, j, i=0):
                    dve.wait_ge(w_hi_done, j * ITEM_SLABS + i * 2 + (S_MOE + c + 1))
                    V.tensor_tensor(w_lo[c % 2][:], raw[c % 2][:], w_hi[c % 2][:].bitcast(F32), ALU.subtract).then_inc(w_lo_done, 1)

                def slots(j):
                    if not isinstance(j, int):
                        dve.wait_ge(slots_turned, j)
                    for t in range(TT):
                        last = V.tensor_scalar(onehot[:, t], iota[:], item_pos[:, t, bass.ds(j, 1)], None, ALU.is_equal)
                    last.then_inc(onehot_ready, 1)

                def gathered(kt, t, j, step):
                    dve.wait_ge(tile_done, j * step + (t + 1))
                    V.tensor_copy(g_hl[:, kt].rearrange("p x c -> p (x c)"), pp[kt % 2][:, 0:2 * CAP]).then_inc(tile_free[kt % 2], 1)

                slots(0)
                for kt in range(KT):
                    gathered(kt, T_MOE + kt, 0, 0)
                lo_item(1, 0)
                with dve.Fori(0, n_items) as j:
                    t = T_ITEM
                    slots(j + 1)
                    with dve.Fori(0, 4) as i:
                        lo_item(2, j, i)
                        for c in range(2):
                            dve.wait_ge(tile_free[c], j * (ITEM_TILES // 2) + i * 2 + (t // 2 + 1))
                            dve.wait_ge(tile_done, j * ITEM_TILES + i * 4 + (t + 2 + c + 1))
                            V.tensor_tensor(tB(c, CAP), pp[(t + c) % 2][:, 0:CAP], tA(c, CAP), ALU.mult
                                            ).then_inc(tile_free[(t + c) % 2], 1)
                        for c in range(2):
                            dve.wait_ge(prod_hi, j * 8 + i * 2 + (P_MOE + c + 1))
                            at = (slice(None), bass.ds(i * 2 + c, 1))
                            V.tensor_tensor(e_lo[at], tB(c, CAP).unsqueeze(1), e_hi[at].bitcast(F32), ALU.subtract).then_inc(prod_lo, 1)
                        lo_item(3, j, i)

                    def next_tokens(*tiles):
                        for kt in tiles:
                            gathered(kt, t + GATHER_AT[kt], j, ITEM_TILES)

                    def outputs(n):
                        for sl in range(2):
                            dve.wait_ge(yhi_done, j * 8 + (2 * n + sl + 1))
                            at = (slice(None), sl, slice(n * SLAB, (n + 1) * SLAB))
                            V.scalar_tensor_tensor(y_lo[at], pp[sl][:, 0:SLAB], gslot[:, sl:sl + 1], y_hi[at].bitcast(F32),
                                                   ALU.mult, ALU.subtract).then_inc(tile_free[sl], 1)

                    next_tokens(0, 1)
                    outputs(0)
                    next_tokens(2, 3)
                    lo_item(10, j)
                    outputs(1)
                    lo_item(11, j)
                    outputs(2)
                    next_tokens(4, 5)
                    lo_item(12, j)
                    outputs(3)
                    next_tokens(6, 7)
                    lo_item(13, j)
                    for d in range(KT):
                        add_tile(t + COMBINE_AT + d, d, NMOD + 40, j, ITEM_TILES)

            V.memset(eps[:], EPS).then_inc(eps_set, 1)
            dve.wait_ge(kept_in, 16)
            step(V.tensor_scalar(sink8[:], kp("sink"), 1 / SCALE, None, ALU.mult))
            lo(0)
            first_mods()
            keep_mods(0, MOD_FIRST)
            norm(0)
            project_in(0)
            keep_mods(16, 16)
            qk_norm(0)
            attention(0)
            project_out(0)
            keep_mods(32, 8)
            norm(1)
            ffn()
            keep_mods(48, 48)
            norm(2)
            project_in(1)
            qk_norm(1)
            attention(1)
            project_out(1)
            norm(3)
            routing()
            experts()


def shape_constants():
    import numpy as np

    f = np.float32
    eye = np.eye(P, dtype=f)
    rot = np.zeros((P, P), f)
    for n in range(P):
        quarter = HD // 4
        if n % (2 * quarter) < quarter:
            rot[n + quarter, n] = -1
        else:
            rot[n - quarter, n] = 1
    blk = np.kron(np.eye(P // HD), np.ones((HD, HD))).astype(f)
    a, b = np.arange(P)[:, None], np.arange(P)[None, :]
    rows = np.repeat(np.arange(LAT // 64, dtype=f), 64)
    cols = np.tile(np.arange(64, dtype=f), LAT // 64)
    inv = f(10000.0) ** (-np.arange(HD // 4, dtype=f) / f(HD // 4))
    ang = np.stack([rows[:, None] * inv, cols[:, None] * inv], axis=1)
    per = np.concatenate([ang[:, 0], ang[:, 0], ang[:, 1], ang[:, 1]], axis=1).T
    per = np.concatenate([per, per], axis=0)
    edge = np.ones((4, 2, 8), f)
    for g in range(4):
        w = 2 << g
        for x in range(8):
            edge[g, 0, x] = f(w) / f(min(w, x + w // 2))
            edge[g, 1, x] = f(w) / f(min(w, w // 2 + 8 - x))
    cand = np.arange(NCAND)
    thr = np.where(cand < NE, -1, CAP * (cand // NE))
    wide = {
        "ident": eye, "ones": np.ones((P, P)), "rot": rot, "blk": blk, "upper": (a < b),
        "mprev": np.where(b >= a, 0, NEG), "mnext": np.where(b <= a, 0, NEG),
        "cos": np.cos(per), "sin": np.sin(per), "edge": edge.reshape(-1), "iota": np.arange(CAP),
        "desc": NE - np.arange(NE), "thr": thr, "cand": cand % NE,
        "u24": (cand[None, :] < cand[:, None]).reshape(-1), "jidx": np.repeat(np.arange(ROOM), NCAND),
    }
    return {n: np.broadcast_to(np.asarray(v, f), (P, np.asarray(v).shape[-1])) for n, v in wide.items()}


def lay_out(x):
    import numpy as np

    f = np.float32
    consts = shape_constants()

    def columns(a):
        return np.ascontiguousarray(a.reshape(-1, P).T)

    def slabs(w, order=None):
        kk, n = w.shape
        w = w.reshape(kk // P, P, n // SLAB, SLAB).transpose(2, 1, 0, 3)
        out = np.zeros((n // SLAB, P, 8, SLAB), f)
        out[:, :, :kk // P] = w
        return out.reshape(n // SLAB, P, 8 * SLAB)

    heads = np.arange(512).reshape(2, 4, HD).transpose(1, 0, 2).reshape(-1)
    ev, od = x["ev_w_in"][0], x["od_w_in"][0]
    bg, cg, xa = ev[:, 0:512], ev[:, 512:1024], ev[:, 1024:1536]
    parts = [slabs(ev[:, 1536 + heads]), slabs(ev[:, 2048:2304])]
    for n in range(2):
        parts += [slabs(w[:, n * SLAB:(n + 1) * SLAB]) for w in (xa, cg, bg)]
    eo, oo = x["ev_w_out"][0], x["od_w_out"][0]
    parts.append(slabs(np.concatenate([eo[512 + heads], eo[0:512]])))
    w1, w3, w2 = x["ffn_w1"][0], x["ffn_w3"][0], x["ffn_w2"][0]
    at = 0
    for hidden in FFN_PARTS:
        for n in range(hidden // 2):
            c = slice(at + n * SLAB, at + (n + 1) * SLAB)
            parts += [slabs(w1[:, c]), slabs(w3[:, c])]
        parts.append(slabs(w2[at:at + hidden * P]))
        at += hidden * P
    parts += [slabs(od[:, heads]), slabs(od[:, 512:1280])]
    parts.append(slabs(np.concatenate([oo[heads], oo[512:]])))
    for e in range(NE):
        a, b = slabs(x["moe_w1"][0, e]), slabs(x["moe_w3"][0, e])
        parts += [np.stack([a, b], axis=1).reshape(8, P, -1), slabs(x["moe_w2"][0, e])]
    ws = np.concatenate(parts)
    wmod = x["w_mod"].transpose(0, 2, 1).reshape(2 * NMOD, P, D)
    cond = np.broadcast_to(np.stack([x["c"][0], x["c_ctx"]]), (P, 2, D))
    tokens = np.concatenate([x["x_sample"][0], x["x_prompt"][0]])
    xT = tokens.T.reshape(KT, P, TOK).transpose(1, 0, 2)

    def gain(a):
        return np.concatenate([a[0], a[0]])[:, None]

    def rows(a):
        return np.broadcast_to(a.reshape(1, -1), (P, a.size))

    kc = x["cache_k"][0].transpose(0, 1, 3, 2).reshape(2, P, PAST).transpose(1, 0, 2).reshape(P, -1)
    vc = x["cache_v"][0].transpose(0, 2, 1, 3).reshape(2, 2, P, P).transpose(2, 0, 1, 3).reshape(P, -1)
    data = {
        "bmod": columns(x["b_mod"]), "norm1": columns(x["norm1"]), "norm2": columns(x["norm2"]),
        "conv": columns(x["ev_conv"][0]), "pscale": columns(x["od_pool_scale"]),
        "gain": np.concatenate([gain(x[n]) for n in ("ev_q_norm", "ev_k_norm", "od_q_norm", "od_k_norm")], axis=1),
        "sink": rows(x["od_sink"]), "rbias": rows(x["moe_router_b"]), "kc": kc, "vc": vc,
        "poolw": x["od_pool_w"][0].transpose(1, 0, 2).reshape(P, -1),
        "router": x["moe_router"][0].reshape(KT, P, NE).transpose(1, 0, 2).reshape(P, -1),
    }
    data.update(consts)

    def pack(table):
        return np.concatenate([data[n] for n, _ in table], axis=1)

    return {"xT": xT, "kept": pack(_KEPT), "mixer": pack(_MIXER), "route": pack(_ROUTE), "iota": data["iota"],
            "cond": cond, "wmod": wmod, "ws": ws}


def kernel(**inputs):
    import numpy as np
    import concourse.bacc as bacc
    from concourse.bass_utils import run_bass_kernel_spmd

    given = {n: np.asarray(a) for n, a in inputs.items()}
    nc = bacc.Bacc("TRN2", target_bir_lowering=False, num_devices=1)
    arrays, args = {}, []
    for name, a in lay_out(given).items():
        a = np.ascontiguousarray(a)
        arrays[f"in_{name}"] = a
        args.append(nc.dram_tensor(f"in_{name}", a.shape, mybir.dt.from_np(a.dtype), kind="ExternalInput").ap())
    for name, shape in (("out_y", (P, KT, TOK)), ("out_k", (2, P, CTX)), ("out_v", (2, P, CTX))):
        args.append(nc.dram_tensor(name, shape, F32, kind="ExternalOutput").ap())
    build(nc, *args)
    got = run_bass_kernel_spmd(nc, [arrays], core_ids=[0]).results[0]
    y = got["out_y"].transpose(2, 1, 0).reshape(TOK, D)
    new_k, new_v = (got[n].reshape(1, 2, 2, HD, CTX).transpose(0, 1, 2, 4, 3) for n in ("out_k", "out_v"))
    return (np.ascontiguousarray(y[None, LAT:]), np.ascontiguousarray(y[None, :LAT]),
            np.ascontiguousarray(new_k), np.ascontiguousarray(new_v))
```
